# Optimizing a Trainium2 kernel written in Bass

```python
import math
import jax, jax.numpy as jnp
from jax import lax
import numpy as np

D_MODEL = 1024
BATCH = 1
SEQ = 256
DEPTH = 1

CTX_LEN = 256
GRID_W = 64
N_MIXERS = 3
CHUNK = 64
Q_BLOCK = 128
EPS = 1e-6

GDN_HEADS = 8
GDN_DK = D_MODEL // GDN_HEADS
GDN_DV = D_MODEL // GDN_HEADS
GDN_CONV = 5
GDN_IN = 2 * GDN_HEADS * GDN_DK + 2 * GDN_HEADS * GDN_DV + 4 * GDN_HEADS

MLSTM_HEADS = 8
MLSTM_DQK = D_MODEL // (2 * MLSTM_HEADS)
MLSTM_DV = D_MODEL // MLSTM_HEADS
MLSTM_IN = 2 * MLSTM_HEADS * MLSTM_DQK + 2 * MLSTM_HEADS * MLSTM_DV + 4 * MLSTM_HEADS

ATTN_HEADS = 8
ATTN_KV_HEADS = 2
ATTN_GROUP = ATTN_HEADS // ATTN_KV_HEADS
ATTN_DH = D_MODEL // ATTN_HEADS
ATTN_IN = (ATTN_HEADS + 2 * ATTN_KV_HEADS) * ATTN_DH
ROPE_THETA = 10000.0

FFN_DIM = ((8 * D_MODEL // 3 + 127) // 128) * 128
FFN_CONV = 3


F32 = jnp.float32

def rms_norm(x, g):
    xf = x.astype(F32)
    y = xf * lax.rsqrt(jnp.mean(xf * xf, axis=-1, keepdims=True) + EPS)
    return (y * g.astype(F32)).astype(x.dtype)

def l2_norm(x):
    xf = x.astype(F32)
    return xf * lax.rsqrt(jnp.sum(xf * xf, axis=-1, keepdims=True) + EPS)

def modulate(h, shift, scale):
    return h * (1.0 + scale) + shift

def dw_conv(x, w):
    k = w.shape[0]
    return lax.conv_general_dilated(
        x, w[:, None, :].astype(x.dtype), window_strides=(1,), padding=[(k // 2, k // 2)],
        dimension_numbers=("NWC", "WIO", "NWC"), feature_group_count=x.shape[-1])

def to_chunks(t):
    b, l, h = t.shape[:3]
    t = t.reshape(b, l // CHUNK, CHUNK, h, *t.shape[3:])
    return jnp.moveaxis(t, (1, 3), (0, 2))

def from_chunks(t):
    t = jnp.moveaxis(t, (0, 2), (1, 3))
    return t.reshape(t.shape[0], t.shape[1] * t.shape[2], *t.shape[3:])

def tri_masks():
    i = jnp.arange(CHUNK)
    return i[:, None] >= i[None, :], i[:, None] > i[None, :]

def flip_seq(t):
    return jnp.flip(t, axis=1)

def identity(t):
    return t

def gated_delta_chunked(q, k, v, beta, g, s0):
    incl, strict = tri_masks()
    q, k, v, beta, g = map(to_chunks, (q, k, v, beta, g))
    gc = jnp.cumsum(g, axis=-1)
    decay = jnp.exp(jnp.where(incl, gc[..., :, None] - gc[..., None, :], -jnp.inf))
    kk = jnp.einsum("nbhid,nbhjd->nbhij", k, k)
    a_mat = jnp.where(strict, beta[..., :, None] * kk * decay, 0.0) + jnp.eye(CHUNK, dtype=kk.dtype)
    rhs = jnp.concatenate([v * beta[..., None], k * (beta * jnp.exp(gc))[..., None]], axis=-1)
    sol = lax.linalg.triangular_solve(a_mat, rhs, left_side=True, lower=True, unit_diagonal=True)
    dv = v.shape[-1]
    u, w = sol[..., :dv], sol[..., dv:]
    qk = jnp.einsum("nbhid,nbhjd->nbhij", q, k) * decay
    q_dec = q * jnp.exp(gc)[..., None]
    k_dec = k * jnp.exp(gc[..., -1:] - gc)[..., None]
    a_last = jnp.exp(gc[..., -1])

    def step(s, xs):
        qd, kd, u_c, w_c, qk_c, al = xs
        v_new = u_c - jnp.einsum("bhck,bhkv->bhcv", w_c, s)
        o = jnp.einsum("bhck,bhkv->bhcv", qd, s) + jnp.einsum("bhij,bhjv->bhiv", qk_c, v_new)
        s = s * al[..., None, None] + jnp.einsum("bhck,bhcv->bhkv", kd, v_new)
        return s, o

    s_fin, o = lax.scan(step, s0, (q_dec, k_dec, u, w, qk, a_last))
    return from_chunks(o), s_fin

def gdn_project(h, w_in, conv_w, a_log, dt_bias):
    bsz, l, _ = h.shape
    nqk, nv = GDN_HEADS * GDN_DK, GDN_HEADS * GDN_DV
    z = h @ w_in
    qkv = jax.nn.silu(dw_conv(z[..., :2 * nqk + nv], conv_w))
    q = l2_norm(qkv[..., :nqk].reshape(bsz, l, GDN_HEADS, GDN_DK)) * (GDN_DK ** -0.5)
    k = l2_norm(qkv[..., nqk:2 * nqk].reshape(bsz, l, GDN_HEADS, GDN_DK))
    v = qkv[..., 2 * nqk:].reshape(bsz, l, GDN_HEADS, GDN_DV).astype(F32)
    gate = z[..., 2 * nqk + nv:2 * nqk + 2 * nv]
    ba = z[..., 2 * nqk + 2 * nv:].reshape(bsz, l, 2, 2, GDN_HEADS).astype(F32)
    beta = jax.nn.sigmoid(ba[:, :, :, 0])
    g = -jnp.exp(a_log.astype(F32)) * jax.nn.softplus(ba[:, :, :, 1] + dt_bias.astype(F32))
    return q, k, v, beta, g, gate

def gdn_mixer(h_ctx, h_lat, want_ctx, w_in, conv_w, a_log, dt_bias, norm_g, w_out):
    qc, kc, vc, bc, gcx, gate_c = gdn_project(h_ctx, w_in, conv_w, a_log, dt_bias)
    ql, kl, vl, bl, glt, gate_l = gdn_project(h_lat, w_in, conv_w, a_log, dt_bias)
    s0 = jnp.zeros((h_ctx.shape[0], GDN_HEADS, GDN_DK, GDN_DV), F32)
    o_ctx, o_lat = [], []
    for d, f in enumerate((identity, flip_seq)):
        oc, s_ctx = gated_delta_chunked(f(qc), f(kc), f(vc), f(bc[:, :, d]), f(gcx[:, :, d]), s0)
        ol, _ = gated_delta_chunked(f(ql), f(kl), f(vl), f(bl[:, :, d]), f(glt[:, :, d]), s_ctx)
        o_ctx.append(f(oc))
        o_lat.append(f(ol))

    def finish(o_pair, gate, dtype):
        o = rms_norm(o_pair[0] + o_pair[1], norm_g)
        o = o.reshape(*o.shape[:2], GDN_HEADS * GDN_DV) * jax.nn.silu(gate.astype(F32))
        return o.astype(dtype) @ w_out

    y_ctx = finish(o_ctx, gate_c, h_ctx.dtype) if want_ctx else None
    return y_ctx, finish(o_lat, gate_l, h_lat.dtype)

def mlstm_chunked(q, k, v, ig, lf, c0, n0, m0):
    incl, _ = tri_masks()
    q, k, v, ig, lf = map(to_chunks, (q, k, v, ig, lf))
    b = jnp.cumsum(lf, axis=-1)
    dlog = jnp.where(incl, b[..., :, None] - b[..., None, :] + ig[..., None, :], -jnp.inf)
    a = jnp.max(dlog, axis=-1)
    p = jnp.exp(dlog - a[..., None]) * jnp.einsum("nbhid,nbhjd->nbhij", q, k)
    num_in = jnp.einsum("nbhij,nbhjv->nbhiv", p, v)
    den_in = jnp.sum(p, axis=-1)
    b_last = b[..., -1]
    wlog = b_last[..., None] - b + ig
    m_loc = jnp.max(wlog, axis=-1)
    kw = k * jnp.exp(wlog - m_loc[..., None])[..., None]
    dc = jnp.einsum("nbhck,nbhcv->nbhkv", kw, v)
    dn = jnp.sum(kw, axis=-2)

    def step(carry, xs):
        cm, nm, mm = carry
        qc, bc, ac, num_c, den_c, bl, ml, dcc, dnc = xs
        m_t = jnp.maximum(ac, bc + mm[..., None])
        s_inter = jnp.exp(bc + mm[..., None] - m_t)
        s_intra = jnp.exp(ac - m_t)
        num = s_inter[..., None] * jnp.einsum("bhck,bhkv->bhcv", qc, cm) + s_intra[..., None] * num_c
        den = s_inter * jnp.einsum("bhck,bhk->bhc", qc, nm) + s_intra * den_c
        h = num / jnp.maximum(jnp.abs(den), jnp.exp(-m_t))[..., None]
        m_new = jnp.maximum(bl + mm, ml)
        f_sc = jnp.exp(bl + mm - m_new)
        i_sc = jnp.exp(ml - m_new)
        cm = f_sc[..., None, None] * cm + i_sc[..., None, None] * dcc
        nm = f_sc[..., None] * nm + i_sc[..., None] * dnc
        return (cm, nm, m_new), h

    (c_f, n_f, m_f), h = lax.scan(step, (c0, n0, m0), (q, b, a, num_in, den_in, b_last, m_loc, dc, dn))
    return from_chunks(h), c_f, n_f, m_f

def mlstm_project(h, w_in, gate_b):
    bsz, l, _ = h.shape
    nqk, nv = MLSTM_HEADS * MLSTM_DQK, MLSTM_HEADS * MLSTM_DV
    z = h @ w_in
    q = z[..., :nqk].reshape(bsz, l, MLSTM_HEADS, MLSTM_DQK).astype(F32) * (MLSTM_DQK ** -0.5)
    k = z[..., nqk:2 * nqk].reshape(bsz, l, MLSTM_HEADS, MLSTM_DQK).astype(F32)
    v = z[..., 2 * nqk:2 * nqk + nv].reshape(bsz, l, MLSTM_HEADS, MLSTM_DV).astype(F32)
    o_gate = z[..., 2 * nqk + nv:2 * nqk + 2 * nv]
    gates = z[..., 2 * nqk + 2 * nv:].reshape(bsz, l, 2, 2, MLSTM_HEADS).astype(F32) + gate_b.astype(F32)
    ig = gates[:, :, :, 0]
    lf = jax.nn.log_sigmoid(gates[:, :, :, 1])
    return q, k, v, ig, lf, o_gate

def mlstm_mixer(h_ctx, h_lat, want_ctx, w_in, gate_b, norm_g, w_out):
    qc, kc, vc, igc, lfc, og_c = mlstm_project(h_ctx, w_in, gate_b)
    ql, kl, vl, igl, lfl, og_l = mlstm_project(h_lat, w_in, gate_b)
    bsz = h_ctx.shape[0]
    c0 = jnp.zeros((bsz, MLSTM_HEADS, MLSTM_DQK, MLSTM_DV), F32)
    n0 = jnp.zeros((bsz, MLSTM_HEADS, MLSTM_DQK), F32)
    m0 = jnp.zeros((bsz, MLSTM_HEADS), F32)
    o_ctx, o_lat = [], []
    for d, f in enumerate((identity, flip_seq)):
        hc, cc, nc, mc = mlstm_chunked(f(qc), f(kc), f(vc), f(igc[:, :, d]), f(lfc[:, :, d]), c0, n0, m0)
        hl, _, _, _ = mlstm_chunked(f(ql), f(kl), f(vl), f(igl[:, :, d]), f(lfl[:, :, d]), cc, nc, mc)
        o_ctx.append(f(hc))
        o_lat.append(f(hl))

    def finish(h_pair, o_gate, dtype):
        o = rms_norm(h_pair[0] + h_pair[1], norm_g)
        o = o.reshape(*o.shape[:2], MLSTM_HEADS * MLSTM_DV) * jax.nn.sigmoid(o_gate.astype(F32))
        return o.astype(dtype) @ w_out

    y_ctx = finish(o_ctx, og_c, h_ctx.dtype) if want_ctx else None
    return y_ctx, finish(o_lat, og_l, h_lat.dtype)

def axial_rope(seq_len):
    rows = seq_len // GRID_W
    row = jnp.repeat(jnp.arange(rows), GRID_W).astype(F32)
    col = jnp.tile(jnp.arange(GRID_W), rows).astype(F32)
    n_pair = ATTN_DH // 4
    inv = ROPE_THETA ** (-jnp.arange(n_pair, dtype=F32) / n_pair)
    ang = jnp.concatenate([row[:, None] * inv, col[:, None] * inv], axis=-1)
    return jnp.cos(ang), jnp.sin(ang)

def apply_rope(x, cos, sin):
    xr = x.reshape(*x.shape[:-1], -1, 2)
    x0, x1 = xr[..., 0], xr[..., 1]
    cos = cos.astype(x.dtype)
    sin = sin.astype(x.dtype)
    return jnp.stack([x0 * cos - x1 * sin, x0 * sin + x1 * cos], axis=-1).reshape(x.shape)

def attend(q, k, v):
    s = jnp.einsum("bqhgd,bkhd->bhgqk", q, k, preferred_element_type=F32) * (ATTN_DH ** -0.5)
    p = jax.nn.softmax(s, axis=-1).astype(v.dtype)
    return jnp.einsum("bhgqk,bkhd->bqhgd", p, v)

def gqa_mixer(h_ctx, h_lat, want_ctx, w_in, q_norm_g, k_norm_g, w_out):
    nq, nk = ATTN_HEADS * ATTN_DH, ATTN_KV_HEADS * ATTN_DH

    def project(h):
        bsz, l, _ = h.shape
        z = h @ w_in
        q = rms_norm(z[..., :nq].reshape(bsz, l, ATTN_KV_HEADS, ATTN_GROUP, ATTN_DH), q_norm_g)
        k = rms_norm(z[..., nq:nq + nk].reshape(bsz, l, ATTN_KV_HEADS, ATTN_DH), k_norm_g)
        v = z[..., nq + nk:].reshape(bsz, l, ATTN_KV_HEADS, ATTN_DH)
        return q, k, v

    qc, kc, vc = project(h_ctx)
    ql, kl, vl = project(h_lat)
    bsz, l = h_lat.shape[:2]
    cos, sin = axial_rope(l)
    ql = apply_rope(ql, cos[:, None, None, :], sin[:, None, None, :])
    kl = apply_rope(kl, cos[:, None, :], sin[:, None, :])
    k_all = jnp.concatenate([kc, kl], axis=1)
    v_all = jnp.concatenate([vc, vl], axis=1)
    nb = l // Q_BLOCK
    qb = jnp.moveaxis(ql.reshape(bsz, nb, Q_BLOCK, ATTN_KV_HEADS, ATTN_GROUP, ATTN_DH), 1, 0)
    ob = lax.map(lambda qq: attend(qq, k_all, v_all), qb)
    y_lat = jnp.moveaxis(ob, 0, 1).reshape(bsz, l, nq) @ w_out
    y_ctx = attend(qc, kc, vc).reshape(bsz, h_ctx.shape[1], nq) @ w_out if want_ctx else None
    return y_ctx, y_lat

def conv_glu(h, w_in, conv_w, conv_b, w_out):
    val, gate = jnp.split(h @ w_in, 2, axis=-1)
    gate = dw_conv(gate, conv_w) + conv_b
    return (val * jax.nn.silu(gate)) @ w_out

def _count(kind):
    return len(range(kind, DEPTH, N_MIXERS))

def first_inputs(seed: int = 0) -> dict:
    key = jax.random.key(seed)
    keys = iter(jax.random.split(key, 40))

    def nrm(shape, std):
        return std * jax.random.normal(next(keys), shape, F32)

    D = D_MODEL
    n_a, n_b, n_c = _count(0), _count(1), _count(2)
    x = nrm((BATCH, SEQ, D), 1.0)
    c = nrm((BATCH, D), 1.0)
    ctx = nrm((BATCH, CTX_LEN, D), 1.0)
    c_ctx = nrm((D,), 1.0)
    norm1_g = 1.0 + nrm((DEPTH, D), 0.02)
    norm2_g = 1.0 + nrm((DEPTH, D), 0.02)
    w_mod = nrm((DEPTH, D, 6 * D), 0.5 * D ** -0.5)
    b_mod = nrm((DEPTH, 6 * D), 0.02)
    ffn_w_in = nrm((DEPTH, D, 2 * FFN_DIM), D ** -0.5)
    ffn_conv_w = nrm((DEPTH, FFN_CONV, FFN_DIM), FFN_CONV ** -0.5)
    ffn_conv_b = nrm((DEPTH, FFN_DIM), 0.02)
    ffn_w_out = nrm((DEPTH, FFN_DIM, D), FFN_DIM ** -0.5)
    gdn_w_in = nrm((n_a, D, GDN_IN), D ** -0.5)
    gdn_conv_w = nrm((n_a, GDN_CONV, 2 * GDN_HEADS * GDN_DK + GDN_HEADS * GDN_DV), GDN_CONV ** -0.5)
    gdn_a_log = jnp.log(jax.random.uniform(next(keys), (n_a, 2, GDN_HEADS), F32, 1.0, 16.0))
    dt = jnp.exp(jax.random.uniform(next(keys), (n_a, 2, GDN_HEADS), F32, math.log(1e-3), math.log(1e-1)))
    gdn_dt_bias = dt + jnp.log(-jnp.expm1(-dt))
    gdn_norm_g = 1.0 + nrm((n_a, GDN_DV), 0.02)
    gdn_w_out = nrm((n_a, GDN_HEADS * GDN_DV, D), (GDN_HEADS * GDN_DV) ** -0.5)
    mlstm_w_in = nrm((n_b, D, MLSTM_IN), D ** -0.5)
    ig_b = nrm((n_b, 2, 1, MLSTM_HEADS), 0.1)
    fg_b = jnp.linspace(3.0, 6.0, MLSTM_HEADS, dtype=F32) + nrm((n_b, 2, 1, MLSTM_HEADS), 0.1)
    mlstm_gate_b = jnp.concatenate([ig_b, fg_b], axis=2)
    mlstm_norm_g = 1.0 + nrm((n_b, MLSTM_DV), 0.02)
    mlstm_w_out = nrm((n_b, MLSTM_HEADS * MLSTM_DV, D), (MLSTM_HEADS * MLSTM_DV) ** -0.5)
    attn_w_in = nrm((n_c, D, ATTN_IN), D ** -0.5)
    attn_q_norm_g = 1.0 + nrm((n_c, ATTN_DH), 0.02)
    attn_k_norm_g = 1.0 + nrm((n_c, ATTN_DH), 0.02)
    attn_w_out = nrm((n_c, ATTN_HEADS * ATTN_DH, D), (ATTN_HEADS * ATTN_DH) ** -0.5)
    final_norm_g = 1.0 + nrm((D,), 0.02)
    return {
        "x": x, "c": c, "ctx": ctx, "c_ctx": c_ctx,
        "norm1_g": norm1_g, "norm2_g": norm2_g, "w_mod": w_mod, "b_mod": b_mod,
        "ffn_w_in": ffn_w_in, "ffn_conv_w": ffn_conv_w, "ffn_conv_b": ffn_conv_b, "ffn_w_out": ffn_w_out,
        "gdn_w_in": gdn_w_in, "gdn_conv_w": gdn_conv_w, "gdn_a_log": gdn_a_log, "gdn_dt_bias": gdn_dt_bias,
        "gdn_norm_g": gdn_norm_g, "gdn_w_out": gdn_w_out,
        "mlstm_w_in": mlstm_w_in, "mlstm_gate_b": mlstm_gate_b, "mlstm_norm_g": mlstm_norm_g,
        "mlstm_w_out": mlstm_w_out,
        "attn_w_in": attn_w_in, "attn_q_norm_g": attn_q_norm_g, "attn_k_norm_g": attn_k_norm_g,
        "attn_w_out": attn_w_out, "final_norm_g": final_norm_g,
    }

def first_block(x, c, ctx, c_ctx, norm1_g, norm2_g, w_mod, b_mod, ffn_w_in, ffn_conv_w, ffn_conv_b,
              ffn_w_out, gdn_w_in, gdn_conv_w, gdn_a_log, gdn_dt_bias, gdn_norm_g, gdn_w_out,
              mlstm_w_in, mlstm_gate_b, mlstm_norm_g, mlstm_w_out, attn_w_in, attn_q_norm_g,
              attn_k_norm_g, attn_w_out, final_norm_g):
    x_lat, x_ctx = x, ctx
    s_lat = jax.nn.silu(c)[:, None, :]
    s_ctx = jax.nn.silu(c_ctx)[None, None, :]
    for i in range(DEPTH):
        last = i == DEPTH - 1
        kind, j = i % N_MIXERS, i // N_MIXERS
        mod_l = jnp.split(s_lat @ w_mod[i] + b_mod[i], 6, axis=-1)
        mod_c = jnp.split(s_ctx @ w_mod[i] + b_mod[i], 6, axis=-1)
        h_lat = modulate(rms_norm(x_lat, norm1_g[i]), mod_l[0], mod_l[1])
        h_ctx = modulate(rms_norm(x_ctx, norm1_g[i]), mod_c[0], mod_c[1])
        if kind == 0:
            y_ctx, y_lat = gdn_mixer(h_ctx, h_lat, not last, gdn_w_in[j], gdn_conv_w[j], gdn_a_log[j],
                                     gdn_dt_bias[j], gdn_norm_g[j], gdn_w_out[j])
        elif kind == 1:
            y_ctx, y_lat = mlstm_mixer(h_ctx, h_lat, not last, mlstm_w_in[j], mlstm_gate_b[j],
                                       mlstm_norm_g[j], mlstm_w_out[j])
        else:
            y_ctx, y_lat = gqa_mixer(h_ctx, h_lat, not last, attn_w_in[j], attn_q_norm_g[j],
                                     attn_k_norm_g[j], attn_w_out[j])
        x_lat = x_lat + mod_l[2] * y_lat
        h_lat = modulate(rms_norm(x_lat, norm2_g[i]), mod_l[3], mod_l[4])
        x_lat = x_lat + mod_l[5] * conv_glu(h_lat, ffn_w_in[i], ffn_conv_w[i], ffn_conv_b[i], ffn_w_out[i])
        if not last:
            x_ctx = x_ctx + mod_c[2] * y_ctx
            h_ctx = modulate(rms_norm(x_ctx, norm2_g[i]), mod_c[3], mod_c[4])
            x_ctx = x_ctx + mod_c[5] * conv_glu(h_ctx, ffn_w_in[i], ffn_conv_w[i], ffn_conv_b[i], ffn_w_out[i])
    return rms_norm(x_lat, final_norm_g)


DEPTH_2 = 2

N_EVEN = (DEPTH_2 + 1) // 2
N_ODD = DEPTH_2 // 2
ALPHA = (2.0 * DEPTH_2) ** 0.25
BETA = (8.0 * DEPTH_2) ** -0.25
LN_EPS = 1e-5

POOL_WINDOWS = (2, 4, 8, 16)
POOL_GROUPS = len(POOL_WINDOWS)
POOL_CH = D_MODEL // 8
POOL_WIDTH = POOL_GROUPS * POOL_CH
HEAD_DIM = 64
N_Q_HEADS = D_MODEL // 128
N_KV_HEADS = 2
Q_GROUP = N_Q_HEADS // N_KV_HEADS
ATTN_WIDTH = N_Q_HEADS * HEAD_DIM
KV_WIDTH = N_KV_HEADS * HEAD_DIM
WINDOW = 128
BLOCK = 128
EVEN_IN = POOL_WIDTH + ATTN_WIDTH + 2 * KV_WIDTH
EVEN_MIX = POOL_WIDTH + ATTN_WIDTH

CHUNK_2 = 128
SG_WIDTH = D_MODEL
SG_GROUPS = 8
SG_CH = SG_WIDTH // SG_GROUPS

D_FF = ((8 * D_MODEL // 3 + 127) // 128) * 128
N_EXPERTS = 8
TOP_K = 2
D_FF_EXPERT = 7 * D_MODEL // 2


def layer_norm(x, g, b):
    xf = x.astype(jnp.float32)
    mu = jnp.mean(xf, axis=-1, keepdims=True)
    var = jnp.mean(jnp.square(xf - mu), axis=-1, keepdims=True)
    return ((xf - mu) * lax.rsqrt(var + LN_EPS) * g + b).astype(x.dtype)

def pool_mixer(p, w_pool, pool_scale):
    B_, S, _ = p.shape
    pf = p.astype(jnp.float32)
    cs = jnp.concatenate([jnp.zeros((B_, 1, POOL_WIDTH), jnp.float32), jnp.cumsum(pf, axis=1)], axis=1)
    t = jnp.arange(S)
    outs = []
    for g, w in enumerate(POOL_WINDOWS):
        r = w // 2
        lo = jnp.maximum(t - r, 0)
        hi = jnp.minimum(t + r + 1, S)
        sl = slice(g * POOL_CH, (g + 1) * POOL_CH)
        csg = cs[..., sl]
        cnt = (hi - lo).astype(jnp.float32)[None, :, None]
        outs.append((csg[:, hi] - csg[:, lo]) / cnt - pf[..., sl])
    pooled = jnp.stack(outs, axis=2).astype(p.dtype)
    y = jnp.einsum('bsgc,gcd->bsgd', pooled, w_pool)
    return y.reshape(B_, S, POOL_WIDTH) * pool_scale

def windowed_gqa(q, k, v, sink):
    B_, S, _, _ = q.shape
    nb = S // BLOCK
    qb = q.reshape(B_, nb, BLOCK, N_KV_HEADS, Q_GROUP, HEAD_DIM)
    pad = ((0, 0), (BLOCK, BLOCK), (0, 0), (0, 0))
    kp = jnp.pad(k, pad).reshape(B_, nb + 2, BLOCK, N_KV_HEADS, HEAD_DIM)
    vp = jnp.pad(v, pad).reshape(B_, nb + 2, BLOCK, N_KV_HEADS, HEAD_DIM)
    kw = jnp.concatenate([kp[:, :-2], kp[:, 1:-1], kp[:, 2:]], axis=2)
    vw = jnp.concatenate([vp[:, :-2], vp[:, 1:-1], vp[:, 2:]], axis=2)
    scores = jnp.einsum('bnqhgd,bnshd->bnhgqs', qb, kw).astype(jnp.float32) * (HEAD_DIM ** -0.5)
    i = jnp.arange(BLOCK)[:, None]
    j = jnp.arange(3 * BLOCK)[None, :]
    dist = jnp.abs(j - BLOCK - i)
    key_pos = jnp.arange(nb)[:, None] * BLOCK - BLOCK + jnp.arange(3 * BLOCK)[None, :]
    valid = (key_pos >= 0) & (key_pos < S)
    mask = (dist <= WINDOW)[None] & valid[:, None, :]
    slopes = 2.0 ** (-8.0 * jnp.arange(1, N_Q_HEADS + 1, dtype=jnp.float32) / N_Q_HEADS)
    alibi = -slopes.reshape(N_KV_HEADS, Q_GROUP)[:, :, None, None] * dist.astype(jnp.float32)
    scores = jnp.where(mask[None, :, None, None], scores + alibi, -1e30)
    sink_b = sink.astype(jnp.float32).reshape(N_KV_HEADS, Q_GROUP)[None, None, :, :, None, None]
    m = jnp.maximum(jnp.max(scores, axis=-1, keepdims=True), sink_b)
    pexp = jnp.exp(scores - m)
    probs = pexp / (jnp.sum(pexp, axis=-1, keepdims=True) + jnp.exp(sink_b - m))
    out = jnp.einsum('bnhgqs,bnshd->bnqhgd', probs.astype(v.dtype), vw)
    return out.reshape(B_, S, ATTN_WIDTH)

def even_mixer(h, w_in, w_pool, pool_scale, sink, w_out):
    B_, S, _ = h.shape
    z = h @ w_in
    p, q, k, v = jnp.split(z, [POOL_WIDTH, POOL_WIDTH + ATTN_WIDTH, POOL_WIDTH + ATTN_WIDTH + KV_WIDTH], axis=-1)
    ya = pool_mixer(p, w_pool, pool_scale)
    yb = windowed_gqa(q.reshape(B_, S, N_Q_HEADS, HEAD_DIM),
                      k.reshape(B_, S, N_KV_HEADS, HEAD_DIM),
                      v.reshape(B_, S, N_KV_HEADS, HEAD_DIM), sink)
    return jnp.concatenate([ya, yb], axis=-1) @ w_out

def spatial_gating_mixer(h, w_in, sg_ln_g, sg_ln_b, w_s, b_s, w_out):
    B_, S, _ = h.shape
    z = jax.nn.gelu(h @ w_in)
    u, v = jnp.split(z, 2, axis=-1)
    v = layer_norm(v, sg_ln_g, sg_ln_b)
    vc = v.reshape(B_, S // CHUNK_2, CHUNK_2, SG_GROUPS, SG_CH)
    sv = jnp.einsum('gts,bnsgc->bntgc', w_s, vc) + b_s.T[None, None, :, :, None]
    return (u * sv.reshape(B_, S, SG_WIDTH)) @ w_out

def swiglu(h, w_gate, w_up, w_down):
    return (jax.nn.silu(h @ w_gate) * (h @ w_up)) @ w_down

def moe_swiglu(h, w_router, w_gate, w_up, w_down):
    logits = (h @ w_router).astype(jnp.float32)
    top_v, top_i = lax.top_k(logits, TOP_K)
    gates = jax.nn.softmax(top_v, axis=-1)
    dense_gate = jnp.sum(jax.nn.one_hot(top_i, N_EXPERTS, dtype=jnp.float32) * gates[..., None], axis=-2)
    y = jnp.zeros_like(h)
    for e in range(N_EXPERTS):
        y = y + dense_gate[..., e:e + 1].astype(h.dtype) * swiglu(h, w_gate[e], w_up[e], w_down[e])
    return y

def second_inputs(seed: int = 0) -> dict:
    key = jax.random.key(seed)
    ks = jax.random.split(key, 32)
    f32 = jnp.float32
    D = D_MODEL

    def nrm(k, shape, scale):
        return jax.random.normal(k, shape, f32) * scale

    x = nrm(ks[0], (BATCH, SEQ, D), 1.0)
    c = nrm(ks[1], (BATCH, D), 1.0)
    ada_w = nrm(ks[2], (DEPTH_2, D, 6 * D), 0.1 * D ** -0.5)
    ada_b = nrm(ks[3], (DEPTH_2, 6 * D), 0.01)
    ln_g = 1.0 + nrm(ks[4], (DEPTH_2, 2, D), 0.02)
    ln_b = nrm(ks[5], (DEPTH_2, 2, D), 0.01)

    ev_w_in = nrm(ks[6], (N_EVEN, D, EVEN_IN), D ** -0.5)
    col_scale = jnp.concatenate([jnp.full((EVEN_IN - KV_WIDTH,), 1.0, f32), jnp.full((KV_WIDTH,), BETA, f32)])
    ev_w_in = ev_w_in * col_scale
    ev_pool_w = nrm(ks[7], (N_EVEN, POOL_GROUPS, POOL_CH, POOL_CH), POOL_CH ** -0.5)
    ev_pool_scale = 1.0 + nrm(ks[8], (N_EVEN, POOL_WIDTH), 0.02)
    ev_sink = nrm(ks[9], (N_EVEN, N_Q_HEADS), 0.5)
    ev_w_out = nrm(ks[10], (N_EVEN, EVEN_MIX, D), BETA * EVEN_MIX ** -0.5)

    od_w_in = nrm(ks[11], (N_ODD, D, 2 * SG_WIDTH), D ** -0.5)
    od_sg_ln_g = 1.0 + nrm(ks[12], (N_ODD, SG_WIDTH), 0.02)
    od_sg_ln_b = nrm(ks[13], (N_ODD, SG_WIDTH), 0.01)
    od_w_s = nrm(ks[14], (N_ODD, SG_GROUPS, CHUNK_2, CHUNK_2), CHUNK_2 ** -0.5)
    od_b_s = 1.0 + nrm(ks[15], (N_ODD, SG_GROUPS, CHUNK_2), 0.02)
    od_w_out = nrm(ks[16], (N_ODD, SG_WIDTH, D), BETA * SG_WIDTH ** -0.5)

    ffn_w_gate = nrm(ks[17], (N_EVEN, D, D_FF), BETA * D ** -0.5)
    ffn_w_up = nrm(ks[18], (N_EVEN, D, D_FF), BETA * D ** -0.5)
    ffn_w_down = nrm(ks[19], (N_EVEN, D_FF, D), BETA * D_FF ** -0.5)

    moe_w_router = nrm(ks[20], (N_ODD, D, N_EXPERTS), D ** -0.5)
    moe_w_gate = nrm(ks[21], (N_ODD, N_EXPERTS, D, D_FF_EXPERT), BETA * D ** -0.5)
    moe_w_up = nrm(ks[22], (N_ODD, N_EXPERTS, D, D_FF_EXPERT), BETA * D ** -0.5)
    moe_w_down = nrm(ks[23], (N_ODD, N_EXPERTS, D_FF_EXPERT, D), BETA * D_FF_EXPERT ** -0.5)

    return {"x": x, "c": c, "ada_w": ada_w, "ada_b": ada_b, "ln_g": ln_g, "ln_b": ln_b,
            "ev_w_in": ev_w_in, "ev_pool_w": ev_pool_w, "ev_pool_scale": ev_pool_scale,
            "ev_sink": ev_sink, "ev_w_out": ev_w_out,
            "od_w_in": od_w_in, "od_sg_ln_g": od_sg_ln_g, "od_sg_ln_b": od_sg_ln_b,
            "od_w_s": od_w_s, "od_b_s": od_b_s, "od_w_out": od_w_out,
            "ffn_w_gate": ffn_w_gate, "ffn_w_up": ffn_w_up, "ffn_w_down": ffn_w_down,
            "moe_w_router": moe_w_router, "moe_w_gate": moe_w_gate, "moe_w_up": moe_w_up,
            "moe_w_down": moe_w_down}

def second_block(x, c, ada_w, ada_b, ln_g, ln_b,
              ev_w_in, ev_pool_w, ev_pool_scale, ev_sink, ev_w_out,
              od_w_in, od_sg_ln_g, od_sg_ln_b, od_w_s, od_b_s, od_w_out,
              ffn_w_gate, ffn_w_up, ffn_w_down,
              moe_w_router, moe_w_gate, moe_w_up, moe_w_down):
    cond = jax.nn.silu(c)
    for l in range(DEPTH_2):
        mod = (cond @ ada_w[l] + ada_b[l])[:, None, :]
        sh_m, sc_m, g_m, sh_f, sc_f, g_f = jnp.split(mod, 6, axis=-1)
        e = l // 2
        h = x * (1.0 + sc_m) + sh_m
        if l % 2 == 0:
            y = even_mixer(h, ev_w_in[e], ev_pool_w[e], ev_pool_scale[e], ev_sink[e], ev_w_out[e])
        else:
            y = spatial_gating_mixer(h, od_w_in[e], od_sg_ln_g[e], od_sg_ln_b[e], od_w_s[e], od_b_s[e], od_w_out[e])
        x = layer_norm(ALPHA * x + (1.0 + g_m) * y, ln_g[l, 0], ln_b[l, 0])
        h = x * (1.0 + sc_f) + sh_f
        if l % 2 == 0:
            y = swiglu(h, ffn_w_gate[e], ffn_w_up[e], ffn_w_down[e])
        else:
            y = moe_swiglu(h, moe_w_router[e], moe_w_gate[e], moe_w_up[e], moe_w_down[e])
        x = layer_norm(ALPHA * x + (1.0 + g_f) * y, ln_g[l, 1], ln_b[l, 1])
    return x


_first_inputs = second_inputs


def second_inputs(seed=0):
    import zlib

    import numpy as np

    out = dict(_first_inputs(seed))
    spreads = {}
    factors = {'ada_b': 6.856,
     'ev_pool_scale': 8.0,
     'ev_sink': 8.0,
     'od_sg_ln_g': 8.0,
     'od_sg_ln_b': 8.0,
     'od_b_s': 8.0}
    for name, (base, spread) in spreads.items():
        noise = np.random.default_rng([zlib.crc32(name.encode()), seed]).standard_normal(out[name].shape)
        drawn = base * np.exp(spread * noise) if base else spread * noise
        out[name] = __import__('jax').numpy.asarray(drawn.astype(out[name].dtype))
    for name, factor in factors.items():
        out[name] = (out[name] * factor).astype(out[name].dtype)
    return out


_narrow_inputs = second_inputs


def second_inputs(seed=0):

    out = dict(_narrow_inputs(seed))
    wider = {'ev_sink': 6.32, 'od_sg_ln_g': 4.78, 'od_sg_ln_b': 9.05, 'od_b_s': 5.03}
    for name, times in wider.items():
        mean = out[name].mean()
        out[name] = (mean + times * (out[name] - mean)).astype(out[name].dtype)
    return out


def setup_inputs(seed=0):
    out = dict(first_inputs(seed))
    for name, value in second_inputs(seed + 1).items():
        if name != "x":
            out[name + "_2"] = value
    return out


def reference(
    x, c, ctx, c_ctx, norm1_g, norm2_g, w_mod, b_mod, ffn_w_in, ffn_conv_w, ffn_conv_b,
    ffn_w_out, gdn_w_in, gdn_conv_w, gdn_a_log, gdn_dt_bias, gdn_norm_g, gdn_w_out, mlstm_w_in,
    mlstm_gate_b, mlstm_norm_g, mlstm_w_out, attn_w_in, attn_q_norm_g, attn_k_norm_g,
    attn_w_out, final_norm_g, c_2, ada_w_2, ada_b_2, ln_g_2, ln_b_2, ev_w_in_2, ev_pool_w_2,
    ev_pool_scale_2, ev_sink_2, ev_w_out_2, od_w_in_2, od_sg_ln_g_2, od_sg_ln_b_2, od_w_s_2,
    od_b_s_2, od_w_out_2, ffn_w_gate_2, ffn_w_up_2, ffn_w_down_2, moe_w_router_2, moe_w_gate_2,
    moe_w_up_2, moe_w_down_2,
):
    x = first_block(
        x, c, ctx, c_ctx, norm1_g, norm2_g, w_mod, b_mod, ffn_w_in, ffn_conv_w, ffn_conv_b,
        ffn_w_out, gdn_w_in, gdn_conv_w, gdn_a_log, gdn_dt_bias, gdn_norm_g, gdn_w_out,
        mlstm_w_in, mlstm_gate_b, mlstm_norm_g, mlstm_w_out, attn_w_in, attn_q_norm_g,
        attn_k_norm_g, attn_w_out, final_norm_g,
    )
    return second_block(
        x, c_2, ada_w_2, ada_b_2, ln_g_2, ln_b_2, ev_w_in_2, ev_pool_w_2, ev_pool_scale_2,
        ev_sink_2, ev_w_out_2, od_w_in_2, od_sg_ln_g_2, od_sg_ln_b_2, od_w_s_2, od_b_s_2,
        od_w_out_2, ffn_w_gate_2, ffn_w_up_2, ffn_w_down_2, moe_w_router_2, moe_w_gate_2,
        moe_w_up_2, moe_w_down_2,
    )


_drawn_inputs = setup_inputs


def setup_inputs(seed=0):
    import zlib

    import numpy as np

    out = dict(_drawn_inputs(seed))
    spreads = {}
    factors = {'c_ctx': 3.822,
     'norm1_g': 7.387,
     'norm2_g': 6.728,
     'ffn_conv_b': 23.424,
     'gdn_norm_g': 8.0,
     'ev_sink_2': 4.418}
    for name, (base, spread) in spreads.items():
        noise = np.random.default_rng([zlib.crc32(name.encode()), seed]).standard_normal(out[name].shape)
        drawn = base * np.exp(spread * noise) if base else spread * noise
        out[name] = __import__('jax').numpy.asarray(drawn.astype(out[name].dtype))
    for name, factor in factors.items():
        out[name] = (out[name] * factor).astype(out[name].dtype)
    return out
```

```python
from contextlib import ExitStack

import numpy as np

import concourse.bass as bass
from concourse import mybir

F32 = mybir.dt.float32
I32 = mybir.dt.int32
ALU = mybir.AluOpType
ACT = mybir.ActivationFunctionType
AX_X = mybir.AxisListType.X

P = 128
D = 1024
KT = D // P
T = 256
TC = 256
TALL = TC + T
EPS = 1e-6
LN_EPS = 1e-5

TILE = 4096
GROUP = TILE // KT
DOWN_ROWS = TILE // D
RING = 5

HEADS = 8
GDN_CONV = 5
CHUNKS = TALL // P
LAT0 = TC // P
LEVELS = (2, 4, 8, 16, 32, 64)
FFN = 2816
FT = FFN // P
FFN_CONV = 3

DEPTH_2 = 2
ALPHA = (2.0 * DEPTH_2) ** 0.25
WINDOWS = (2, 4, 8, 16)
Q_HEADS = 8
HEAD = 64
KV_HEADS = 2
SLOPES = [2.0 ** (-8.0 * (h + 1) / Q_HEADS) for h in range(Q_HEADS)]
WINDOW = 128
FAR = 1e33
SG_GROUPS = 8
EXPERTS = 8
EXPERT_FFN = 3584



PARAMS_1 = dict(cond=KT * 3, b_mod=48, norm1_g=KT, norm2_g=KT, final_g=KT, conv_w=GDN_CONV * 24, ffn_conv_w=FFN_CONV * FT,
                ffn_conv_b=FT, gdn_norm_g=1, a_log=16, dt_bias=16, w_ba=KT * 32)


def offsets(sizes):
    at, out = 0, {}
    for name, n in sizes.items():
        out[name] = slice(at, at + n)
        at += n
    return out, at


PARAMS_2 = dict(ada_b=2 * 48, ln_g=4 * KT, ln_b=4 * KT, pool_scale=4, sink=Q_HEADS, sg_g=KT, sg_b=KT, b_s=SG_GROUPS * P,
                w_s=SG_GROUPS * P, pool_w=4 * P, w_router=KT * EXPERTS)
COLS, N_COLS = offsets(PARAMS_1)
COLS_2, N_COLS_2 = offsets(PARAMS_2)

CONSTS = dict(ident=P, ones=P, incl0=P, incl1=P, strict0=P, strict1=P,
              **{f"merge{s}_{d}": P for s in (1,) + LEVELS for d in range(2)})
CCOLS, N_CONSTS = offsets(CONSTS)
N_CONSTS_2 = 4 * 2 * T + 2 * T + EXPERTS * EXPERTS


def constants_2():
    s, t = np.arange(T)[:, None], np.arange(T)[None, :]
    parts = []
    for w in WINDOWS:
        lo, hi = np.maximum(t - w // 2, 0), np.minimum(t + w // 2 + 1, T)
        band = ((s >= lo) & (s < hi)) / (hi - lo) - (s == t)
        parts.append(rows_tile(band))
    dist = np.abs(s - t).astype(np.float64)
    parts.append(rows_tile(np.where(dist <= WINDOW, dist, FAR)))
    e = np.arange(EXPERTS)
    parts.append(np.broadcast_to((e[None, :] < e[:, None]).reshape(1, -1), (P, EXPERTS * EXPERTS)))
    return np.concatenate(parts, axis=1).astype(np.float32)


def constants():
    i, j = np.arange(P)[:, None], np.arange(P)[None, :]
    m = dict(ident=i == j, ones=i == i + 0 * j, incl0=i >= j, incl1=i <= j, strict0=i > j, strict1=i < j)
    for s in (1,) + LEVELS:
        low = (i // (2 * s) == j // (2 * s)) & (i // s > j // s)
        m[f"merge{s}_0"], m[f"merge{s}_1"] = low, low.T
    return np.concatenate([np.broadcast_to(m[k], (P, P)) for k in CONSTS], axis=1).astype(np.float32)


def groups(width):
    return [(c, min(GROUP, width - c)) for c in range(0, width, GROUP)]



def column_tiles(width):
    return [n * KT for _, n in groups(width)]


def ffn_tiles(width):
    out = []
    for _, n in groups(width):
        out += [n * KT, n * KT, n // P * D]
    return out


def stream_plan():
    return (column_tiles(6 * D) * 3 + column_tiles(4 * D) + column_tiles(D) + ffn_tiles(FFN)
            + column_tiles(D) + [3 * P * KT] + column_tiles(D) + ffn_tiles(FFN)
            + column_tiles(2 * D) + column_tiles(D) + ffn_tiles(EXPERT_FFN) * EXPERTS)


class WeightStream:

    def __init__(self, plan, ring, dram, tile_loaded, tile_used):
        self.plan, self.ring, self.dram, self.tile_loaded, self.tile_used = plan, ring, dram, tile_loaded, tile_used
        self.issued = 0
        self.taken = 0
        self.due = 0

    def issue(self, sp, upto):
        while self.issued < min(upto, len(self.plan)):
            n = self.issued
            if n >= RING:
                sp.wait_ge(self.tile_used, n - RING + 1)
            words = self.plan[n]
            sp.dma_start(self.ring[:, n % RING, 0:words], self.dram[n, :, 0:words]).then_inc(self.tile_loaded[n % RING], 16)
            self.issued += 1

    def take(self, pe):
        n = self.taken
        pe.wait_ge(self.tile_loaded[n % RING], 16 * (n // RING + 1))
        self.taken += 1
        return self.ring[:, n % RING, :]


    def release(self, n=1):
        self.due += n

    def tell(self, mm):
        if self.due:
            mm.then_inc(self.tile_used, self.due)
            self.due = 0


class Counted:

    def __init__(self, sem):
        self.sem, self.base, self.told = sem, 0, 0

    def at(self, n):
        return self.sem, self.base + n

    def up(self, n):
        self.told += n
        return self.sem


class Chain:

    def __init__(self, eng, steps):
        self.eng, self.steps, self.n = eng, steps, 0

    def __call__(self, ins):
        self.n += 1
        ins.then_inc(self.steps.up(1), 1)
        self.eng.wait_ge(*self.steps.at(self.n))



class Core:

    def __init__(self, nc, ctx, weights, plan):
        self.nc, self.ctx, self.counts = nc, ctx, {}
        self.arena = ctx.enter_context(nc.sbuf_tensor("arena", [P, 32512], F32))
        self.ps = ctx.enter_context(nc.psum_tensor("ps", [P, 8, 512], F32))
        ring = ctx.enter_context(nc.sbuf_tensor("ring", [P, RING, TILE], F32))
        self.w = WeightStream(plan, ring, weights, [self.sem(f"tile_loaded{i}") for i in range(RING)], self.sem("tile_used"))
        self.at = 0
        self.consts = self.take(N_CONSTS)

    def sem(self, name):
        return self.ctx.enter_context(self.nc.semaphore(name))

    def counted(self, name):
        s = self.counts.setdefault(name, None) or Counted(self.sem(name))
        self.counts[name] = s
        s.base, s.told = s.base + s.told, 0
        return s

    def take(self, *shape):
        n = int(np.prod(shape))
        a = self.arena[:, self.at:self.at + n]
        self.at += n
        assert self.at <= 32512, self.at
        if len(shape) == 2:
            a = a.rearrange("p (a b) -> p a b", a=shape[0])
        if len(shape) == 3:
            a = a.rearrange("p (a b c) -> p a b c", a=shape[0], b=shape[1])
        if len(shape) == 4:
            a = a.rearrange("p (a b c d) -> p a b c d", a=shape[0], b=shape[1], c=shape[2])
        return a

    def const(self, name):
        return self.consts[:, CCOLS[name]]

    def col(self, name, *shape):
        a = self.cols[:, self.cols_of[name]]
        if len(shape) == 2:
            a = a.rearrange("p (a b) -> p a b", a=shape[0])
        return a


def over(ap, n):
    return ap.unsqueeze(1).to_broadcast([P, n, ap.shape[1]])


def along(ap, n):
    return ap.unsqueeze(2).to_broadcast([P, ap.shape[1], n])


def load_inputs(core, loads):
    nc = core.nc
    landed = core.sem("inputs_landed")
    with nc.Block(no_gpsimd_drain=True) as block:
        @block.sync
        def _(sp):
            core.w.issue(sp, RING)

        @block.scalar
        def _(act):
            for dst, src in loads:
                act.dma_start(dst, src).then_inc(landed, 16)
            act.wait_ge(landed, 16 * len(loads))


def conditioning(core, name, rhs, n_rhs, bias, mod):
    nc, w = core.nc, core.w
    sums_ready = core.counted("sums_ready")
    with nc.Block(no_gpsimd_drain=True) as block:
        @block.sync
        def _(sp):
            w.issue(sp, w.taken + 12 + RING)

        @block.tensor
        def _(pe):
            for g in range(12):
                tile = w.take(pe).rearrange("p (k c) -> p k c", k=KT)
                for f in range(4 * g, 4 * g + 4):
                    for k in range(KT):
                        mm = nc.tensor.matmul(core.ps[:, 0, f * n_rhs:(f + 1) * n_rhs], tile[:, k, (f % 4) * P:(f % 4 + 1) * P],
                                              rhs[:, k, 0:n_rhs], start=(k == 0), stop=(k == KT - 1))
                mm.then_inc(w.tile_used, 1)

        @block.vector
        def _(dve):
            dve.wait_ge(w.tile_used, w.taken)
            nc.vector.tensor_tensor(mod, core.ps[:, 0, 0:48 * n_rhs].rearrange("p (f r) -> p f r", r=n_rhs),
                                    along(bias, n_rhs), ALU.add).then_inc(sums_ready.up(1), 1)


def column_norm(core, name, src, dst, sq, stat, eps, affine, centred):
    nc = core.nc
    n = src.shape[2]
    squares_ready, sums_ready, mean_ready, centred_ready, var_ready, root_ready, chain = (
        core.counted(s) for s in ("squares_ready", "sums_ready", "mean_ready", "centred_ready", "var_ready", "root_ready", "chain"))
    body = dst if centred else src
    with nc.Block(no_gpsimd_drain=True) as block:
        @block.tensor
        def _(pe):
            if centred:
                for k in range(KT):
                    mm = nc.tensor.matmul(core.ps[:, 0, 0:n], core.const("ones"), src[:, k], start=(k == 0), stop=(k == KT - 1))
                mm.then_inc(mean_ready.up(1), 1)
            for k in range(KT):
                pe.wait_ge(*squares_ready.at(k + 1))
                mm = nc.tensor.matmul(core.ps[:, 1, 0:n], core.const("ones"), sq[:, k], start=(k == 0), stop=(k == KT - 1))
            mm.then_inc(sums_ready.up(1), 1)

        @block.scalar
        def _(act):
            for k in range(KT):
                if centred:
                    act.wait_ge(*centred_ready.at(k + 1))
                nc.scalar.activation(sq[:, k], body[:, k], ACT.Square).then_inc(squares_ready.up(1), 1)
            act.wait_ge(*var_ready.at(1))
            nc.scalar.activation(stat, stat, ACT.Sqrt).then_inc(root_ready.up(1), 1)

        @block.vector
        def _(dve):
            done = Chain(dve, chain)
            if centred:
                dve.wait_ge(*mean_ready.at(1))
                done(nc.vector.tensor_scalar(stat, core.ps[:, 0, 0:n], 1.0 / D, None, ALU.mult))
                for k in range(KT):
                    nc.vector.tensor_tensor(dst[:, k], src[:, k], stat, ALU.subtract).then_inc(centred_ready.up(1), 1)
            dve.wait_ge(*sums_ready.at(1))
            nc.vector.tensor_scalar(stat, core.ps[:, 1, 0:n], 1.0 / D, eps, ALU.mult, ALU.add).then_inc(var_ready.up(1), 1)
            dve.wait_ge(*root_ready.at(1))
            done(nc.vector.reciprocal(stat, stat))
            if centred:
                dve.wait_ge(*centred_ready.at(KT))
            for k in range(KT):
                done(nc.vector.tensor_tensor(dst[:, k], body[:, k], stat, ALU.mult))
            for k in range(KT):
                for tokens, scale, shift in affine(k):
                    x = dst[:, k, tokens]
                    if shift is None:
                        ins = nc.vector.tensor_scalar(x, x, scale, None, ALU.mult)
                    else:
                        ins = nc.vector.tensor_scalar(x, x, scale, shift, ALU.mult, ALU.add)
                    ins.then_inc(chain.up(1), 1)


def project(core, name, rhs, width, finish, banks=4, on="vector"):
    nc, w = core.nc, core.w
    sums_ready, sums_used = core.counted("sums_ready"), core.counted("sums_used")
    n = rhs.shape[2]
    with nc.Block(no_gpsimd_drain=True) as block:
        @block.sync
        def _(sp):
            w.issue(sp, w.taken + len(groups(width)) + RING)

        @block.tensor
        def _(pe):
            for c, cols in groups(width):
                tile = w.take(pe)[:, 0:KT * cols].rearrange("p (k c) -> p k c", k=KT)
                for f in range(c // P, (c + cols) // P):
                    if f >= banks:
                        pe.wait_ge(*sums_used.at(f - banks + 1))
                    for k in range(KT):
                        mm = nc.tensor.matmul(core.ps[:, f % banks, 0:n], tile[:, k, f * P - c:f * P - c + P], rhs[:, k],
                                              start=(k == 0), stop=(k == KT - 1))
                        if k == 0:
                            w.tell(mm)
                    mm.then_inc(sums_ready.up(1), 1)
                w.release()
            pe.wait_ge(*sums_ready.at(width // P))
            w.tell(pe.nop())

        @(block.vector if on == "vector" else block.scalar)
        def _(eng):
            for f in range(width // P):
                eng.wait_ge(*sums_ready.at(f + 1))
                finish(eng, f, core.ps[:, f % banks, 0:n]).then_inc(sums_used.up(1), 1)


def gdn_project(core, h, q, k, v, gate, gates, pad, taps):
    nc, w = core.nc, core.w
    sums_ready, sums_used, pad_zero, padded, pad_used, conved, conv_used, gates_ready, chain = (
        core.counted(s) for s in ("sums_ready", "sums_used", "pad_zero", "padded", "pad_used", "conved", "conv_used", "gates_ready", "chain"))
    conv_w = core.col("conv_w", GDN_CONV, 24)
    w_ba = core.col("w_ba", KT, 32)

    def segments(f):
        return (1,) if f < HEADS or f >= 3 * HEADS else (0, 1)

    with nc.Block(no_gpsimd_drain=True) as block:
        @block.sync
        def _(sp):
            w.issue(sp, w.taken + 8 + RING)

        @block.tensor
        def _(pe):
            for g in range(8):
                tile = w.take(pe).rearrange("p (k c) -> p k c", k=KT)
                for f in range(4 * g, 4 * g + 4):
                    if f >= 4:
                        pe.wait_ge(*sums_used.at(f - 3))
                    first = TC * segments(f)[0]
                    for kk in range(KT):
                        mm = nc.tensor.matmul(core.ps[:, f % 4, first:TALL], tile[:, kk, (f % 4) * P:(f % 4 + 1) * P],
                                              h[:, kk, first:TALL], start=(kk == 0), stop=(kk == KT - 1))
                        if kk == 0:
                            w.tell(mm)
                    mm.then_inc(sums_ready.up(1), 1)
                w.release()
            for c in range(CHUNKS):
                for kk in range(KT):
                    mm = nc.tensor.matmul(core.ps[:, 4, c * 32:(c + 1) * 32], h[:, kk, c * P:(c + 1) * P], w_ba[:, kk],
                                          start=(kk == 0), stop=(kk == KT - 1))
                    if kk == 0:
                        w.tell(mm)
            mm.then_inc(gates_ready.up(1), 1)

        @block.scalar
        def _(act):
            act.wait_ge(*pad_zero.at(1))
            for f in range(33):
                if f < 32:
                    act.wait_ge(*sums_ready.at(f + 1))
                if f < 24:
                    if f >= 4:
                        act.wait_ge(*pad_used.at(f - 3))
                    for s in segments(f):
                        ins = nc.scalar.activation(pad[:, f % 4, s, 2:2 + T], core.ps[:, f % 4, s * T:(s + 1) * T], ACT.Copy)
                    ins.then_inc(padded.up(1), 1)
                    act.wait_ge(*padded.at(f + 1))
                    act.nop().then_inc(sums_used.up(1), 1)
                elif f < 32:
                    nc.scalar.activation(gate[:, f - 24], core.ps[:, f % 4, TC:TALL], ACT.Silu).then_inc(sums_used.up(1), 1)
                if 1 <= f < 25:
                    e = f - 1
                    act.wait_ge(*conved.at(e + 1))
                    dst = (q, k, v)[e // HEADS][:, e % HEADS]
                    for s in segments(e):
                        d = dst if e < HEADS else dst[:, s * T:(s + 1) * T]
                        ins = nc.scalar.activation(d, taps[:, e % 2, s], ACT.Silu)
                    ins.then_inc(conv_used.up(1), 1)

        @block.vector
        def _(dve):
            nc.vector.memset(pad, 0.0).then_inc(pad_zero.up(1), 1)
            done = Chain(dve, chain)
            for f in range(24):
                dve.wait_ge(*padded.at(f + 1))
                if f >= 2:
                    dve.wait_ge(*conv_used.at(f - 1))
                a, b = segments(f)[0], 2
                x, y = pad[:, f % 4, a:b], taps[:, f % 2, a:b]
                done(nc.vector.tensor_scalar(y, x[:, :, 0:T], conv_w[:, 0, f:f + 1], None, ALU.mult))
                for i in range(1, GDN_CONV):
                    ins = nc.vector.scalar_tensor_tensor(y, x[:, :, i:i + T], conv_w[:, i, f:f + 1], y, ALU.mult, ALU.add)
                    if i < GDN_CONV - 1:
                        done(ins)
                ins.then_inc(conved.up(1), 1)
                dve.wait_ge(*conved.at(f + 1))
                dve.nop().then_inc(pad_used.up(1), 1)
            dve.wait_ge(*gates_ready.at(1))
            nc.vector.tensor_copy(gates, core.ps[:, 4, 0:CHUNKS * 32].rearrange("p (c g) -> p c g", c=CHUNKS)).then_inc(chain.up(1), 1)


def gdn_gates(core, gates, beta, nbeta, kb_scale, kd_scale, alast, gc, g, tmp):
    nc = core.nc
    to_act, to_dve, sums_ready, g_ready, chain, achain = (core.counted(s) for s in ("to_act", "to_dve", "sums_ready", "g_ready", "chain", "achain"))
    raw = gates.rearrange("p c (d j h) -> p j d h c", d=2, j=2)
    z, e, r, ea = tmp
    n = HEADS * CHUNKS

    def flat(ap, d):
        return ap[:, d].rearrange("p h c -> p (h c)")

    with nc.Block(no_gpsimd_drain=True) as block:
        @block.vector
        def _(dve):
            done = Chain(dve, chain)
            dt = core.col("dt_bias", 2, HEADS)
            for d in range(2):
                done(nc.vector.tensor_tensor(z[:, d], raw[:, 1, d], along(dt[:, d], CHUNKS), ALU.add))
            done(nc.vector.tensor_scalar(r, z, 0.0, None, ALU.max))
            done(nc.vector.scalar_tensor_tensor(z, r, -2.0, z, ALU.mult, ALU.add))
            dve.nop().then_inc(to_act.up(1), 1)
            dve.wait_ge(*to_dve.at(1))
            done(nc.vector.tensor_tensor(r, r, e, ALU.add))
            for d in range(2):
                done(nc.vector.tensor_tensor(g[:, d], r[:, d], along(ea[:, d * HEADS:(d + 1) * HEADS], CHUNKS), ALU.mult))
            done(nc.vector.tensor_scalar(g, g, -1.0, None, ALU.mult))
            dve.nop().then_inc(g_ready.up(1), 1)
            dve.wait_ge(*sums_ready.at(1))
            for d in range(2):
                done(nc.vector.tensor_copy(flat(gc, d), core.ps[:, 0, d * n:(d + 1) * n]))
                done(nc.vector.tensor_copy(flat(alast, d), core.ps[:, 1, d * n:(d + 1) * n]))
            done(nc.vector.tensor_tensor(kd_scale, alast, gc, ALU.subtract))
            dve.nop().then_inc(to_act.up(1), 1)
            dve.wait_ge(*to_dve.at(2))
            done(nc.vector.tensor_tensor(kb_scale, kb_scale, beta, ALU.mult))
            done(nc.vector.tensor_scalar(nbeta, beta, -1.0, None, ALU.mult))

        @block.tensor
        def _(pe):
            pe.wait_ge(*g_ready.at(1))
            for d in range(2):
                nc.tensor.matmul(core.ps[:, 0, d * n:(d + 1) * n], core.const(f"incl{1 - d}"), flat(g, d), start=True, stop=True)
                mm = nc.tensor.matmul(core.ps[:, 1, d * n:(d + 1) * n], core.const("ones"), flat(g, d), start=True, stop=True)
            mm.then_inc(sums_ready.up(1), 1)

        @block.scalar
        def _(act):
            done = Chain(act, achain)
            for d in range(2):
                done(nc.scalar.activation(beta[:, d], raw[:, 0, d], ACT.Sigmoid))
            done(nc.scalar.activation(ea, core.col("a_log"), ACT.Exp))
            act.wait_ge(*to_act.at(1))
            done(nc.scalar.activation(e, z, ACT.Exp))
            done(nc.scalar.activation(e, e, ACT.Ln, bias=1.0))
            act.nop().then_inc(to_dve.up(1), 1)
            act.wait_ge(*to_act.at(2))
            done(nc.scalar.activation(kb_scale, gc, ACT.Exp))
            done(nc.scalar.activation(kd_scale, kd_scale, ACT.Exp))
            done(nc.scalar.activation(alast, alast, ACT.Exp))
            act.nop().then_inc(to_dve.up(1), 1)


def inverse_norms(core, name, x, out, sq, eps, div):
    nc = core.nc
    squares_ready, sums_ready, var_ready, root_ready, chain = (core.counted(s) for s in ("squares_ready", "sums_ready", "var_ready", "root_ready", "chain"))
    heads, n = x.shape[1], x.shape[2]
    with nc.Block(no_gpsimd_drain=True) as block:
        @block.tensor
        def _(pe):
            for h in range(heads):
                pe.wait_ge(*squares_ready.at(h + 1))
                if h >= 4:
                    pe.wait_ge(*var_ready.at(h - 3))
                nc.tensor.matmul(core.ps[:, h % 4, 0:n], core.const("ones"), sq[:, h % 2], start=True, stop=True).then_inc(sums_ready.up(1), 1)

        @block.scalar
        def _(act):
            for h in range(heads):
                if h >= 2:
                    act.wait_ge(*sums_ready.at(h - 1))
                nc.scalar.activation(sq[:, h % 2], x[:, h], ACT.Square).then_inc(squares_ready.up(1), 1)
            for h in range(heads):
                act.wait_ge(*var_ready.at(h + 1))
                nc.scalar.activation(out[:, h], out[:, h], ACT.Sqrt).then_inc(root_ready.up(1), 1)

        @block.vector
        def _(dve):
            for h in range(heads):
                dve.wait_ge(*sums_ready.at(h + 1))
                nc.vector.tensor_scalar(out[:, h], core.ps[:, h % 4, 0:n], 1.0 / div, eps, ALU.mult, ALU.add).then_inc(var_ready.up(1), 1)
            for h in range(heads):
                dve.wait_ge(*root_ready.at(h + 1))
                nc.vector.reciprocal(out[:, h], out[:, h]).then_inc(chain.up(1), 1)


def gdn_heads(core, q, k, v, beta, nbeta, kb_scale, kd_scale, alast, gc, g, out, spare):
    nc = core.nc
    S = {s: core.counted(s) for s in (
        "start", "qkv", "rows", "k_rows", "bv", "kkqk", "tri_g", "gsum", "scaled", "edge", "decay", "lower", "lower_t", "lower_tsb",
        "seeds", "seeds_id", "t", "t_sb", "p", "merged", "wt", "wt_sb", "v", "v_sb", "ds", "state", "o", "qk_masked", "qk_t", "qk_tsb",
        "qd", "exp_g", "dve_chain", "act_chain", "pool_chain")}
    kh, vh, qh, kr = core.take(TALL), core.take(TALL), core.take(T), core.take(CHUNKS, P)
    bv, kb, kd = (core.take(2, CHUNKS, P) for _ in range(3))
    low, lowt, x, y = (spare[:, 2 * n:2 * n + 2].rearrange("p d (c n) -> p d c n", c=CHUNKS) for n in range(4))
    t, wt = core.take(2, CHUNKS, P), core.take(2, CHUNKS, P)
    tg, e = t, wt
    qkm, qkt, qd = (core.take(2, 2, P) for _ in range(3))
    vn, state = core.take(2, P), core.take(2, P)
    ps = core.ps
    NL = len(LEVELS)
    order = ((0, 1, 2, 3), (1, 0, 3, 2))

    def bank(b):
        return ps[:, b].rearrange("p (c n) -> p c n", c=CHUNKS)

    with nc.Block(no_gpsimd_drain=True) as block:
        @block.tensor
        def _(pe):
            mm = nc.tensor.matmul
            for h in range(HEADS):
                pe.wait_ge(*S["qkv"].at(h + 1))
                for c in range(CHUNKS):
                    nc.tensor.transpose(bank(0)[:, c], kh[:, c * P:(c + 1) * P], core.const("ident"))
                for c in range(CHUNKS):
                    last = nc.tensor.transpose(bank(1)[:, c], vh[:, c * P:(c + 1) * P], core.const("ident"))
                last.then_inc(S["rows"].up(1), 1)
                for c in range(CHUNKS):
                    kc = kh[:, c * P:(c + 1) * P]
                    last = mm(bank(2)[:, c], kc, kc, start=True, stop=True)
                for c in range(2):
                    last = mm(bank(3)[:, c], qh[:, c * P:(c + 1) * P], kh[:, (LAT0 + c) * P:(LAT0 + c + 1) * P], start=True, stop=True)
                last.then_inc(S["kkqk"].up(1), 1)
                for d in range(2):
                    pe.wait_ge(*S["tri_g"].at(2 * h + d + 1))
                    mm(ps[:, 4 + d], core.const("ones"), tg[:, d].rearrange("p a b -> p (a b)"), start=True, stop=True).then_inc(S["gsum"].up(1), 1)
                for d in range(2):
                    pe.wait_ge(*S["qk_masked"].at(2 * h + d + 1))
                    for c in range(2):
                        last = nc.tensor.transpose(bank(6 + d)[:, c], qkm[:, d, c], core.const("ident"))
                    last.then_inc(S["qk_t"].up(1), 1)
                for d in range(2):
                    pe.wait_ge(*S["lower"].at(2 * h + d + 1))
                    if d == 0:
                        pe.wait_ge(*S["k_rows"].at(h + 1))
                        pe.wait_ge(*S["bv"].at(2 * h + 2))
                    for c in range(CHUNKS):
                        last = nc.tensor.transpose(bank(d)[:, c], low[:, d, c], core.const("ident"))
                    last.then_inc(S["lower_t"].up(1), 1)
                for n in range(NL):
                    for d in range(2):
                        pe.wait_ge(*S["seeds"].at(2 * h + d + 1))
                        if n:
                            pe.wait_ge(*S["merged"].at(2 * NL * h + 2 * (n - 1) + d + 1))
                        for c in range(CHUNKS):
                            last = mm(bank(2 + d)[:, c], lowt[:, d, c], x[:, d, c], start=True, stop=True)
                        last.then_inc(S["t"].up(1), 1)
                    for d in range(2):
                        pe.wait_ge(*S["t_sb"].at(2 * NL * h + 2 * n + d + 1))
                        for c in range(CHUNKS):
                            if n < NL - 1:
                                mm(bank(4 + d)[:, c], y[:, d, c], t[:, d, c], start=True, stop=True)
                        for c in range(CHUNKS):
                            last = mm(bank(d)[:, c], t[:, d, c], y[:, d, c], start=True, stop=True)
                        last.then_inc(S["p"].up(1), 1)
                pe.wait_ge(*S["scaled"].at(4 * h + 4))
                for d in range(2):
                    pe.wait_ge(*S["merged"].at(2 * NL * h + 2 * (NL - 1) + d + 1))
                    for c in range(CHUNKS):
                        last = mm(bank(2 + d)[:, c], kb[:, d, c], y[:, d, c], start=True, stop=True)
                    last.then_inc(S["wt"].up(1), 1)
                for n in range(CHUNKS):
                    for d in range(2):
                        c = order[d][n]
                        if n == 0:
                            pe.wait_ge(*S["merged"].at(2 * NL * (h + 1)))
                        last = mm(bank(d)[:, n], y[:, d, c], bv[:, d, c], start=True, stop=(n == 0))
                        if n:
                            pe.wait_ge(*S["wt_sb"].at(2 * h + d + 1))
                            pe.wait_ge(*S["state"].at(6 * h + 2 * (n - 1) + d + 1))
                            last = mm(bank(d)[:, n], wt[:, d, c], state[:, d], start=False, stop=True)
                        last.then_inc(S["v"].up(1), 1)
                    for d in range(2):
                        c = order[d][n]
                        if c >= LAT0:
                            if n == LAT0:
                                pe.wait_ge(*S["qk_tsb"].at(2 * h + 2))
                                pe.wait_ge(*S["qd"].at(2 * h + 2))
                            mm(bank(6 + d)[:, c - LAT0], state[:, d], qd[:, d, c - LAT0], start=True, stop=False)
                        pe.wait_ge(*S["v_sb"].at(8 * h + 2 * n + d + 1))
                        if c >= LAT0:
                            mm(bank(6 + d)[:, c - LAT0], vn[:, d], qkt[:, d, c - LAT0], start=False, stop=True).then_inc(S["o"].up(1), 1)
                        if n < CHUNKS - 1:
                            mm(bank(4 + d)[:, n], kd[:, d, c], vn[:, d], start=True, stop=True).then_inc(S["ds"].up(1), 1)

        @block.scalar
        def _(act):
            done = Chain(act, S["act_chain"])
            for h in range(HEADS):
                act.wait_ge(*S["rows"].at(h + 1))
                nc.scalar.activation(kr, bank(0), ACT.Copy).then_inc(S["k_rows"].up(1), 1)
                for d in range(2):
                    act.wait_ge(*S["gsum"].at(2 * h + d + 1))
                    nc.scalar.activation(qd[:, d].rearrange("p a b -> p (a b)"), ps[:, 4 + d, TC:TALL], ACT.Exp).then_inc(S["exp_g"].up(1), 1)
                    act.wait_ge(*S["edge"].at(2 * h + d + 1))
                    nc.scalar.activation(e[:, d], e[:, d], ACT.Exp, scale=-1.0).then_inc(S["decay"].up(1), 1)
                for d in range(2):
                    act.wait_ge(*S["qk_t"].at(2 * h + d + 1))
                    nc.scalar.activation(qkt[:, d], bank(6 + d)[:, 0:2], ACT.Copy).then_inc(S["qk_tsb"].up(1), 1)
                for d in range(2):
                    act.wait_ge(*S["lower_t"].at(2 * h + d + 1))
                    nc.scalar.activation(lowt[:, d], bank(d), ACT.Copy).then_inc(S["lower_tsb"].up(1), 1)
                for n in range(NL):
                    for d in range(2):
                        act.wait_ge(*S["t"].at(2 * NL * h + 2 * n + d + 1))
                        nc.scalar.activation(t[:, d], bank(2 + d), ACT.Copy).then_inc(S["t_sb"].up(1), 1)
                for d in range(2):
                    act.wait_ge(*S["wt"].at(2 * h + d + 1))
                    nc.scalar.activation(wt[:, d], bank(2 + d), ACT.Copy, scale=-1.0).then_inc(S["wt_sb"].up(1), 1)
                for n in range(CHUNKS):
                    for d in range(2):
                        act.wait_ge(*S["v"].at(8 * h + 2 * n + d + 1))
                        if n:
                            act.wait_ge(*S["ds"].at(6 * h + 2 * (n - 1) + d + 1))
                        nc.scalar.activation(vn[:, d], bank(d)[:, n], ACT.Copy).then_inc(S["v_sb"].up(1), 1)

        @block.gpsimd
        def _(pool):
            for h in range(HEADS):
                if h:
                    pool.wait_ge(*S["start"].at(h))
                for d in range(2):
                    tri = over(core.const(f"incl{1 - d}"), CHUNKS)
                    nc.gpsimd.tensor_tensor(tg[:, d], tri, along(g[:, d, h], P), ALU.mult).then_inc(S["tri_g"].up(1), 1)
                for d in range(2):
                    nc.gpsimd.tensor_copy(x[:, d], over(core.const("ident"), CHUNKS)).then_inc(S["seeds_id"].up(1), 1)
                    nc.gpsimd.tensor_copy(y[:, d], over(core.const("ident"), CHUNKS)).then_inc(S["seeds_id"].up(1), 1)
                pool.wait_ge(*S["k_rows"].at(h + 1))
                for d in range(2):
                    nc.gpsimd.tensor_tensor(kb[:, d], kr, along(kb_scale[:, d, h], P), ALU.mult).then_inc(S["scaled"].up(1), 1)
                    nc.gpsimd.tensor_tensor(kd[:, d], kr, along(kd_scale[:, d, h], P), ALU.mult).then_inc(S["scaled"].up(1), 1)

        @block.vector
        def _(dve):
            done = Chain(dve, S["dve_chain"])

            def merge(dst, mask, src):
                return nc.vector.copy_predicated(dst, over(core.const(mask), CHUNKS).bitcast(I32), src)

            for h in range(HEADS):
                done(nc.vector.tensor_copy(kh, k[:, h]))
                done(nc.vector.tensor_copy(vh, v[:, h]))
                done(nc.vector.tensor_scalar(qh, q[:, h], float(P) ** -0.5, None, ALU.mult))
                dve.nop().then_inc(S["qkv"].up(1), 1)
                dve.wait_ge(*S["rows"].at(h + 1))
                for d in range(2):
                    dve.wait_ge(*S["rows"].at(h + 1))
                    nc.vector.tensor_tensor(bv[:, d], bank(1), along(beta[:, d, h], P), ALU.mult).then_inc(S["bv"].up(1), 1)
                for d in range(2):
                    dve.wait_ge(*S["exp_g"].at(2 * h + d + 1))
                    for c in range(CHUNKS):
                        ins = nc.vector.tensor_scalar(e[:, d, c], bank(4 + d)[:, c], gc[:, d, h, c:c + 1], 0.0, ALU.subtract, ALU.max)
                    ins.then_inc(S["edge"].up(1), 1)
                for d in range(2):
                    dve.wait_ge(*S["decay"].at(2 * h + d + 1))
                    done(nc.vector.tensor_tensor(e[:, d], e[:, d], over(core.const(f"incl{d}"), CHUNKS), ALU.mult))
                    dve.wait_ge(*S["kkqk"].at(h + 1))
                    nc.vector.tensor_tensor(qkm[:, d], bank(3)[:, 0:2], e[:, d, LAT0:CHUNKS], ALU.mult).then_inc(S["qk_masked"].up(1), 1)
                    for c in range(CHUNKS):
                        ins = nc.vector.scalar_tensor_tensor(low[:, d, c], bank(2)[:, c], nbeta[:, d, h, c:c + 1], e[:, d, c], ALU.mult, ALU.mult)
                    done(ins)
                    done(nc.vector.tensor_tensor(low[:, d], low[:, d], over(core.const(f"strict{d}"), CHUNKS), ALU.mult))
                    dve.nop().then_inc(S["lower"].up(1), 1)
                for d in range(2):
                    dve.wait_ge(*S["exp_g"].at(2 * h + d + 1))
                    nc.vector.tensor_tensor(qd[:, d].rearrange("p a b -> p (a b)"), qd[:, d].rearrange("p a b -> p (a b)"), qh, ALU.mult).then_inc(S["qd"].up(1), 1)
                dve.wait_ge(*S["seeds_id"].at(4 * h + 4))
                for d in range(2):
                    dve.wait_ge(*S["lower_tsb"].at(2 * h + d + 1))
                    done(merge(x[:, d], f"merge1_{d}", low[:, d]))
                    done(merge(y[:, d], f"merge1_{1 - d}", lowt[:, d]))
                    dve.nop().then_inc(S["seeds"].up(1), 1)
                for n, s in enumerate(LEVELS):
                    for d in range(2):
                        dve.wait_ge(*S["p"].at(2 * NL * h + 2 * n + d + 1))
                        if n < NL - 1:
                            done(merge(x[:, d], f"merge{s}_{d}", bank(4 + d)))
                        done(merge(y[:, d], f"merge{s}_{1 - d}", bank(d)))
                        dve.nop().then_inc(S["merged"].up(1), 1)
                for n in range(CHUNKS - 1):
                    for d in range(2):
                        c = order[d][n]
                        dve.wait_ge(*S["ds"].at(6 * h + 2 * n + d + 1))
                        if n == 0:
                            nc.vector.tensor_copy(state[:, d], bank(4 + d)[:, 0]).then_inc(S["state"].up(1), 1)
                        else:
                            if n == LAT0:
                                dve.wait_ge(*S["o"].at(4 * h + d + 1))
                            nc.vector.scalar_tensor_tensor(state[:, d], state[:, d], alast[:, d, h, c:c + 1], bank(4 + d)[:, n],
                                                           ALU.mult, ALU.add).then_inc(S["state"].up(1), 1)
                        dve.wait_ge(*S["state"].at(6 * h + 2 * n + d + 1))
                dve.wait_ge(*S["o"].at(4 * h + 4))
                o = out[:, h].rearrange("p (c n) -> p c n", c=2)
                done(nc.vector.tensor_copy(o, bank(6)[:, 0:2]))
                done(nc.vector.tensor_tensor(o, bank(7)[:, 0:2], o, ALU.add))
                dve.nop().then_inc(S["start"].up(1), 1)


def ffn(core, name, rhs, plan, act_buf, finish, conv=None, gates=None):
    nc, w = core.nc, core.w
    S = {s: core.counted(s) for s in ("up_ready", "up_used", "gated", "act_ready", "act_used", "pad_zero", "padded", "conved", "chain")}
    tiles = sum(n for _, n in plan) // P
    banks = 4

    def acc(m):
        return core.ps[:, 4 + m // 2, (m % 2) * T:(m % 2 + 1) * T]

    with nc.Block(no_gpsimd_drain=True) as block:
        @block.sync
        def _(sp):
            w.issue(sp, w.taken + 3 * len(plan) + RING)

        @block.tensor
        def _(pe):
            down_tiles = {}

            def up(f, first, second, j, last):
                if f >= banks:
                    pe.wait_ge(*S["act_ready"].at(f - banks + 1))
                for half, tile in ((0, first), (1, second)):
                    for k in range(KT):
                        mm = nc.tensor.matmul(core.ps[:, f % banks, half * T:(half + 1) * T], tile[:, k, j * P:(j + 1) * P], rhs[:, k],
                                              start=(k == 0), stop=(k == KT - 1))
                        if k == 0:
                            w.tell(mm)
                mm.then_inc(S["up_ready"].up(1), 1)
                if last:
                    w.release(2)

            def down(f):
                tile, j, last = down_tiles.pop(f)
                pe.wait_ge(*S["act_ready"].at(f + 1))
                for m in range(KT):
                    mm = nc.tensor.matmul(acc(m), tile[:, j, m * P:(m + 1) * P], act_buf[:, f % 2], start=(f == 0 and m % 2 == 0),
                                          stop=(f == tiles - 1), skip_group_check=True)
                    if m == 0:
                        w.tell(mm)
                mm.then_inc(S["act_used"].up(1), 1)
                if last:
                    w.release()

            for c, cols in plan:
                n = cols // P
                first = w.take(pe)[:, 0:KT * cols].rearrange("p (k c) -> p k c", k=KT)
                second = w.take(pe)[:, 0:KT * cols].rearrange("p (k c) -> p k c", k=KT)
                for j in range(n):
                    f = c // P + j
                    up(f, first, second, j, j == n - 1)
                    if f:
                        down(f - 1)
                    if j == 0:
                        third = w.take(pe)[:, 0:n * D].rearrange("p (j c) -> p j c", j=n)
                    down_tiles[f] = (third, j, j == n - 1)
            down(tiles - 1)
            pe.wait_ge(*S["act_used"].at(tiles))
            w.tell(pe.nop())

        @block.scalar
        def _(act):
            if conv:
                pad, taps, bias, cv = conv
                act.wait_ge(*S["pad_zero"].at(1))
            for f in range(tiles):
                act.wait_ge(*S["up_ready"].at(f + 1))
                if conv:
                    if f >= 2:
                        act.wait_ge(*S["conved"].at(f - 1))
                    nc.scalar.activation(pad[:, f % 2, 1:1 + T], core.ps[:, f % banks, T:2 * T], ACT.Copy).then_inc(S["padded"].up(1), 1)
                    act.wait_ge(*S["conved"].at(f + 1))
                    nc.scalar.activation(cv[:, f % 2], cv[:, f % 2], ACT.Silu).then_inc(S["gated"].up(1), 1)
                else:
                    if f >= 2:
                        act.wait_ge(*S["act_used"].at(f - 1))
                    nc.scalar.activation(act_buf[:, f % 2], core.ps[:, f % banks, 0:T], ACT.Silu).then_inc(S["gated"].up(1), 1)

        @block.vector
        def _(dve):
            done = Chain(dve, S["chain"])
            if conv:
                nc.vector.memset(conv[0], 0.0).then_inc(S["pad_zero"].up(1), 1)
            for f in range(tiles):
                buf = act_buf[:, f % 2]
                if conv:
                    pad, taps, bias, cv = conv
                    dve.wait_ge(*S["padded"].at(f + 1))
                    y = cv[:, f % 2]
                    done(nc.vector.tensor_scalar(y, pad[:, f % 2, 0:T], taps[:, 0, f:f + 1], bias[:, f:f + 1], ALU.mult, ALU.add))
                    done(nc.vector.scalar_tensor_tensor(y, pad[:, f % 2, 1:1 + T], taps[:, 1, f:f + 1], y, ALU.mult, ALU.add))
                    nc.vector.scalar_tensor_tensor(y, pad[:, f % 2, 2:2 + T], taps[:, 2, f:f + 1], y, ALU.mult, ALU.add).then_inc(S["conved"].up(1), 1)
                    dve.wait_ge(*S["gated"].at(f + 1))
                    if f >= 2:
                        dve.wait_ge(*S["act_used"].at(f - 1))
                    nc.vector.tensor_tensor(buf, core.ps[:, f % banks, 0:T], y, ALU.mult).then_inc(S["act_ready"].up(1), 1)
                else:
                    dve.wait_ge(*S["gated"].at(f + 1))
                    if gates is not None:
                        done(nc.vector.tensor_tensor(buf, buf, gates(f), ALU.mult))
                    nc.vector.tensor_tensor(buf, core.ps[:, f % banks, T:2 * T], buf, ALU.mult).then_inc(S["act_ready"].up(1), 1)
            dve.wait_ge(*S["act_used"].at(tiles))
            for m in range(KT):
                finish(dve, m, acc(m)).then_inc(S["chain"].up(1), 1)


def first_block(core, x, hall, mod, cond):
    nc = core.nc
    base = core.at
    g1 = core.take(KT, 2)
    prepare = core.counted("chain")
    with nc.Block(no_gpsimd_drain=True) as block:
        @block.vector
        def _(dve):
            done = Chain(dve, prepare)
            done(nc.vector.tensor_scalar(g1, mod[:, 8:16], 1.0, None, ALU.add))
            done(nc.vector.tensor_tensor(g1, g1, along(core.col("norm1_g"), 2), ALU.mult))
    gate = core.take(KT, T)
    gates = core.take(CHUNKS, 32)
    mark = core.at
    h = core.take(KT, TALL)
    mark_h = core.at
    sq, stat = core.take(KT, TALL), core.take(TALL)
    column_norm(core, "norm1", hall, h, sq, stat, EPS, lambda k: [
        (slice(0, TC), g1[:, k, 1:2], mod[:, k, 1:2]), (slice(TC, TALL), g1[:, k, 0:1], mod[:, k, 0:1])], False)
    core.at = mark_h
    q, k, v = core.take(HEADS, T), core.take(HEADS, TALL), core.take(HEADS, TALL)
    mark_qkv = core.at
    pad, taps = core.take(4, 2, T + 4), core.take(2, 2, T)
    gdn_project(core, h, q, k, v, gate, gates, pad, taps)
    core.at = mark_qkv
    mark_heads = core.at
    rq, rk = core.take(HEADS, T), core.take(HEADS, TALL)
    sq2 = core.take(2, TALL)
    inverse_norms(core, "qnorm", q, rq, sq2[:, :, 0:T], EPS, 1.0)
    inverse_norms(core, "knorm", k, rk, sq2, EPS, 1.0)
    normed = core.counted("qk_normed")
    with nc.Block(no_gpsimd_drain=True) as block:
        @block.vector
        def _(dve):
            nc.vector.tensor_tensor(q, q, rq, ALU.mult).then_inc(normed.up(1), 1)
            nc.vector.tensor_tensor(k, k, rk, ALU.mult).then_inc(normed.up(1), 1)
    core.at = mark_heads
    out = q
    beta, nbeta, kb_scale, kd_scale, alast, gc, g = (core.take(2, HEADS, CHUNKS) for _ in range(7))
    tmp = [core.take(2, HEADS, CHUNKS) for _ in range(3)] + [core.take(2 * HEADS)]
    gdn_gates(core, gates, beta, nbeta, kb_scale, kd_scale, alast, gc, g, tmp)
    gdn_heads(core, q, k, v, beta, nbeta, kb_scale, kd_scale, alast, gc, g, out, h)
    core.at = mark_qkv
    ro, sq2, o = core.take(HEADS, T), core.take(2, T), core.take(HEADS, T)
    inverse_norms(core, "onorm", out, ro, sq2, EPS, float(P))
    gated = core.counted("chain")
    with nc.Block(no_gpsimd_drain=True) as block:
        @block.vector
        def _(dve):
            done = Chain(dve, gated)
            for hh in range(HEADS):
                done(nc.vector.tensor_tensor(o[:, hh], out[:, hh], ro[:, hh], ALU.mult))
                done(nc.vector.scalar_tensor_tensor(o[:, hh], o[:, hh], core.col("gdn_norm_g"), gate[:, hh], ALU.mult, ALU.mult))
    project(core, "gdn_out", o, D, lambda dve, f, sums: nc.vector.scalar_tensor_tensor(
        x[:, f], sums, mod[:, 16 + f, 0:1], x[:, f], ALU.mult, ALU.add))
    core.at = base
    g2 = core.take(KT)
    prepare2 = core.counted("chain")
    with nc.Block(no_gpsimd_drain=True) as block:
        @block.vector
        def _(dve):
            done = Chain(dve, prepare2)
            done(nc.vector.tensor_scalar(g2, mod[:, 32:40, 0], 1.0, None, ALU.add))
            done(nc.vector.tensor_tensor(g2, g2, core.col("norm2_g"), ALU.mult))
    h2, sq, stat = core.take(KT, T), core.take(KT, T), core.take(T)
    column_norm(core, "norm2", x, h2, sq, stat, EPS, lambda k: [(slice(0, T), g2[:, k:k + 1], mod[:, 24 + k, 0:1])], False)
    act_buf, pad, cv = core.take(2, T), core.take(2, T + 2), core.take(2, T)
    ffn(core, "conv_glu", h2, groups(FFN), act_buf, lambda dve, m, sums: nc.vector.scalar_tensor_tensor(
        x[:, m], sums, mod[:, 40 + m, 0:1], x[:, m], ALU.mult, ALU.add),
        (pad, core.col("ffn_conv_w", FFN_CONV, FT), core.col("ffn_conv_b"), cv))
    column_norm(core, "final", x, x, sq, stat, EPS, lambda k: [(slice(0, T), core.col("final_g")[:, k:k + 1], None)], False)
    core.at = base


def modulate(core, name, x, h, mod, scale_at, shift_at):
    nc = core.nc
    g = core.take(KT)
    chain = core.counted("chain")
    with nc.Block(no_gpsimd_drain=True) as block:
        @block.vector
        def _(dve):
            done = Chain(dve, chain)
            done(nc.vector.tensor_scalar(g, mod[:, scale_at:scale_at + KT, 0], 1.0, None, ALU.add))
            for k in range(KT):
                done(nc.vector.tensor_scalar(h[:, k], x[:, k], g[:, k:k + 1], mod[:, shift_at + k, 0:1], ALU.mult, ALU.add))
            done(nc.vector.tensor_scalar(x, x, ALPHA, None, ALU.mult))
            at = shift_at + 2 * KT
            done(nc.vector.tensor_scalar(mod[:, at:at + KT], mod[:, at:at + KT], 1.0, None, ALU.add))


def residual(core, x, mod, gate_at):
    nc = core.nc
    return lambda dve, f, sums: nc.vector.scalar_tensor_tensor(x[:, f], sums, mod[:, gate_at + f, 0:1], x[:, f], ALU.mult, ALU.add)


def layer_norm(core, name, x, which, sq, stat):
    g, b = core.col("ln_g", 4, KT), core.col("ln_b", 4, KT)
    column_norm(core, name, x, x, sq, stat, LN_EPS, lambda k: [(slice(0, T), g[:, which, k:k + 1], b[:, which, k:k + 1])], True)


def even_inputs(core, h, prow, qt, kt, vrow):
    nc, w = core.nc, core.w
    sums_ready, drained = core.counted("sums_ready"), core.counted("drained")
    with nc.Block(no_gpsimd_drain=True) as block:
        @block.sync
        def _(sp):
            w.issue(sp, w.taken + 3 + RING)

        @block.tensor
        def _(pe):
            tile = w.take(pe).rearrange("p (k c) -> p k c", k=KT)
            for s in range(2):
                for k in range(KT):
                    mm = nc.tensor.matmul(core.ps[:, s], h[:, k, s * P:(s + 1) * P], tile[:, k], start=(k == 0), stop=(k == KT - 1))
                mm.then_inc(sums_ready.up(1), 1)
            w.release()
            tile = w.take(pe).rearrange("p (k c) -> p k c", k=KT)
            for f in range(4):
                for k in range(KT):
                    mm = nc.tensor.matmul(core.ps[:, 2 + f, 0:T], tile[:, k, f * P:(f + 1) * P], h[:, k], start=(k == 0), stop=(k == KT - 1))
                    if k == 0:
                        w.tell(mm)
                mm.then_inc(sums_ready.up(1), 1)
            w.release()
            tile = w.take(pe)[:, 0:3 * P * KT].rearrange("p (k c) -> p k c", k=KT)
            for f in range(2):
                for k in range(KT):
                    mm = nc.tensor.matmul(core.ps[:, 6, f * T:(f + 1) * T], tile[:, k, f * P:(f + 1) * P], h[:, k], start=(k == 0), stop=(k == KT - 1))
                    if k == 0:
                        w.tell(mm)
            mm.then_inc(sums_ready.up(1), 1)
            for s in range(2):
                for k in range(KT):
                    mm = nc.tensor.matmul(core.ps[:, 7, s * P:(s + 1) * P], h[:, k, s * P:(s + 1) * P], tile[:, k, 2 * P:3 * P],
                                          start=(k == 0), stop=(k == KT - 1))
            mm.then_inc(sums_ready.up(1), 1)
            w.release()
            pe.wait_ge(*sums_ready.at(8))
            w.tell(pe.nop())

        @block.scalar
        def _(act):
            for s in range(2):
                act.wait_ge(*sums_ready.at(s + 1))
                nc.scalar.activation(prow[:, s], core.ps[:, s], ACT.Copy).then_inc(drained.up(1), 1)
            for f in range(4):
                act.wait_ge(*sums_ready.at(3 + f))
                nc.scalar.activation(qt[:, f], core.ps[:, 2 + f, 0:T], ACT.Copy, scale=HEAD ** -0.5).then_inc(drained.up(1), 1)
            act.wait_ge(*sums_ready.at(7))
            nc.scalar.activation(kt, core.ps[:, 6].rearrange("p (a b) -> p a b", a=2), ACT.Copy).then_inc(drained.up(1), 1)
            act.wait_ge(*sums_ready.at(8))
            nc.scalar.activation(vrow, core.ps[:, 7, 0:T].rearrange("p (a b) -> p a b", a=2), ACT.Copy).then_inc(drained.up(1), 1)


def pooling(core, prow, band, pooled, mix):
    nc = core.nc
    pool_ready, pool_sb, map_ready, mapped = (core.counted(s) for s in ("pool_ready", "pool_sb", "map_ready", "mapped"))
    pool_w, scale = core.col("pool_w", 4, P), core.col("pool_scale")
    with nc.Block(no_gpsimd_drain=True) as block:
        @block.tensor
        def _(pe):
            for g in range(4):
                for s in range(2):
                    mm = nc.tensor.matmul(core.ps[:, g, 0:T], prow[:, s, g * P:(g + 1) * P], band[:, g, s], start=(s == 0), stop=(s == 1))
                mm.then_inc(pool_ready.up(1), 1)
            for g in range(4):
                pe.wait_ge(*pool_sb.at(g + 1))
                nc.tensor.matmul(core.ps[:, 4 + g, 0:T], pool_w[:, g], pooled[:, g], start=True, stop=True).then_inc(map_ready.up(1), 1)

        @block.scalar
        def _(act):
            for g in range(4):
                act.wait_ge(*pool_ready.at(g + 1))
                nc.scalar.activation(pooled[:, g], core.ps[:, g, 0:T], ACT.Copy).then_inc(pool_sb.up(1), 1)

        @block.vector
        def _(dve):
            for g in range(4):
                dve.wait_ge(*map_ready.at(g + 1))
                nc.vector.tensor_scalar(mix[:, g], core.ps[:, 4 + g, 0:T], scale[:, g:g + 1], None, ALU.mult).then_inc(mapped.up(1), 1)


def attention(core, qt, kt, vrow, dist, mix):
    nc = core.nc
    S = {s: core.counted(s) for s in ("scores", "max", "exp", "probs", "probs_t", "probs_tsb", "out", "out_sb", "chain", "act_chain")}
    s_all, pt = core.take(2, 2, T), core.take(2, 2, T)
    m, total, edge = core.take(2, 2), core.take(2, 2), core.take(2, 2)
    sink = core.col("sink")

    def rows(h):
        return slice(HEAD * (h % 2), HEAD * (h % 2) + HEAD)

    with nc.Block(no_gpsimd_drain=True) as block:
        @block.tensor
        def _(pe):
            def scores(h):
                if h >= 2:
                    pe.wait_ge(*S["max"].at(h - 1))
                for b in range(2):
                    mm = nc.tensor.matmul(core.ps[:, h % 2, b * T:(b + 1) * T], qt[rows(h), h // 2, b * P:(b + 1) * P],
                                          kt[rows(h), h // (Q_HEADS // KV_HEADS)], start=True, stop=True)
                mm.then_inc(S["scores"].up(1), 1)

            scores(0)
            for h in range(Q_HEADS):
                if h + 1 < Q_HEADS:
                    scores(h + 1)
                pe.wait_ge(*S["probs"].at(h + 1))
                if h >= 2:
                    pe.wait_ge(*S["probs_tsb"].at(h - 1))
                for key in range(2):
                    for b in range(2):
                        tr = nc.tensor.transpose(core.ps[:, 2 + h % 2, key * T + b * P:key * T + (b + 1) * P],
                                                 s_all[:, h % 2, b, key * P:(key + 1) * P], core.const("ident"))
                tr.then_inc(S["probs_t"].up(1), 1)
                pe.wait_ge(*S["probs_tsb"].at(h + 1))
                if h >= 2:
                    pe.wait_ge(*S["out_sb"].at(h - 1))
                g = h // (Q_HEADS // KV_HEADS)
                for key in range(2):
                    mm = nc.tensor.matmul(core.ps[rows(h), 4 + h % 2, 0:T], vrow[:, key, g * HEAD:(g + 1) * HEAD], pt[:, h % 2, key],
                                          start=(key == 0), stop=(key == 1))
                mm.then_inc(S["out"].up(1), 1)

        @block.vector
        def _(dve):
            done = Chain(dve, S["chain"])
            for h in range(Q_HEADS):
                s = s_all[:, h % 2]
                dve.wait_ge(*S["scores"].at(h + 1))
                if h >= 2:
                    dve.wait_ge(*S["probs_t"].at(h - 1))
                done(nc.vector.scalar_tensor_tensor(s, dist, -SLOPES[h], core.ps[:, h % 2].rearrange("p (a b) -> p a b", a=2),
                                                    ALU.mult, ALU.add))
                mh = m[:, h % 2]
                done(nc.vector.tensor_reduce(mh, s, AX_X, ALU.max))
                nc.vector.tensor_scalar(mh, mh, sink[:, h:h + 1], -1.0, ALU.max, ALU.mult).then_inc(S["max"].up(1), 1)
                dve.wait_ge(*S["exp"].at(h + 1))
                th = total[:, h % 2]
                done(nc.vector.tensor_tensor(th, th, edge[:, h % 2], ALU.add))
                done(nc.vector.reciprocal(th, th))
                for b in range(2):
                    ins = nc.vector.tensor_scalar(s[:, b], s[:, b], th[:, b:b + 1], None, ALU.mult)
                ins.then_inc(S["probs"].up(1), 1)

        @block.scalar
        def _(act):
            done = Chain(act, S["act_chain"])

            def finish(h):
                act.wait_ge(*S["probs_t"].at(h + 1))
                if h >= 2:
                    act.wait_ge(*S["out"].at(h - 1))
                nc.scalar.activation(pt[:, h % 2], core.ps[:, 2 + h % 2].rearrange("p (a b) -> p a b", a=2), ACT.Copy).then_inc(S["probs_tsb"].up(1), 1)
                act.wait_ge(*S["out"].at(h + 1))
                nc.scalar.activation(mix[rows(h), 4 + h // 2], core.ps[rows(h), 4 + h % 2, 0:T], ACT.Copy).then_inc(S["out_sb"].up(1), 1)

            for h in range(Q_HEADS):
                act.wait_ge(*S["max"].at(h + 1))
                for b in range(2):
                    done(nc.scalar.activation(s_all[:, h % 2, b], s_all[:, h % 2, b], ACT.Exp, bias=m[:, h % 2, b:b + 1],
                                              accum_out=total[:, h % 2, b:b + 1]))
                nc.scalar.activation(edge[:, h % 2], m[:, h % 2], ACT.Exp, bias=sink[:, h:h + 1]).then_inc(S["exp"].up(1), 1)
                if h:
                    finish(h - 1)
            finish(Q_HEADS - 1)


def spatial_gate(core, u, v, vrow):
    nc = core.nc
    turned, rows_sb, mixed, biased, chain = (core.counted(s) for s in ("turned", "rows_sb", "mixed", "biased", "chain"))
    w_s, b_s = core.col("w_s", SG_GROUPS, P), core.col("b_s", SG_GROUPS, P)
    tmp = core.take(2, 2, P)
    with nc.Block(no_gpsimd_drain=True) as block:
        @block.tensor
        def _(pe):
            for g in range(SG_GROUPS):
                if g >= 4:
                    pe.wait_ge(*rows_sb.at(g - 3))
                for n in range(2):
                    tr = nc.tensor.transpose(core.ps[:, g % 4, n * P:(n + 1) * P], v[:, g, n * P:(n + 1) * P], core.const("ident"))
                tr.then_inc(turned.up(1), 1)
            for g in range(SG_GROUPS):
                pe.wait_ge(*rows_sb.at(g + 1))
                if g >= 4:
                    pe.wait_ge(*biased.at(g - 3))
                for n in range(2):
                    mm = nc.tensor.matmul(core.ps[:, 4 + g % 4, n * P:(n + 1) * P], vrow[:, g, n], w_s[:, g], start=True, stop=True)
                mm.then_inc(mixed.up(1), 1)

        @block.scalar
        def _(act):
            for g in range(SG_GROUPS):
                act.wait_ge(*turned.at(g + 1))
                nc.scalar.activation(vrow[:, g], core.ps[:, g % 4, 0:T].rearrange("p (a b) -> p a b", a=2), ACT.Copy).then_inc(rows_sb.up(1), 1)

        @block.vector
        def _(dve):
            for g in range(SG_GROUPS):
                dve.wait_ge(*mixed.at(g + 1))
                y = core.ps[:, 4 + g % 4, 0:T].rearrange("p (a b) -> p a b", a=2)
                nc.vector.tensor_tensor(tmp[:, g % 2], y, over(b_s[:, g], 2), ALU.add).then_inc(biased.up(1), 1)
                dve.wait_ge(*biased.at(g + 1))
                ug = u[:, g].rearrange("p (a b) -> p a b", a=2)
                nc.vector.tensor_tensor(ug, ug, tmp[:, g % 2], ALU.mult).then_inc(chain.up(1), 1)


def route(core, h, earlier, gates):
    nc = core.nc
    logits_ready, shifted, exp_ready, chain = (core.counted(s) for s in ("logits_ready", "shifted", "exp_ready", "chain"))
    w_r = core.col("w_router", KT, EXPERTS)
    logits, rank, p = core.take(2, EXPERTS), core.take(2, EXPERTS), core.take(2, EXPERTS)
    beat, same = core.take(EXPERTS, EXPERTS), core.take(EXPERTS, EXPERTS)
    top, total = core.take(2), core.take(2)
    with nc.Block(no_gpsimd_drain=True) as block:
        @block.tensor
        def _(pe):
            for s in range(2):
                for k in range(KT):
                    mm = nc.tensor.matmul(core.ps[:, 0, s * EXPERTS:(s + 1) * EXPERTS], h[:, k, s * P:(s + 1) * P], w_r[:, k],
                                          start=(k == 0), stop=(k == KT - 1))
            mm.then_inc(logits_ready.up(1), 1)

        @block.vector
        def _(dve):
            done = Chain(dve, chain)
            dve.wait_ge(*logits_ready.at(1))
            done(nc.vector.tensor_copy(logits, core.ps[:, 0, 0:2 * EXPERTS].rearrange("p (a b) -> p a b", a=2)))
            done(nc.vector.tensor_reduce(top, logits, AX_X, ALU.max))
            nc.vector.tensor_tensor(p, logits, along(top, EXPERTS), ALU.subtract).then_inc(shifted.up(1), 1)
            for s in range(2):
                mine, other = along(logits[:, s], EXPERTS), over(logits[:, s], EXPERTS)
                done(nc.vector.tensor_tensor(same, other, mine, ALU.is_equal))
                done(nc.vector.tensor_tensor(same, same, earlier, ALU.mult))
                done(nc.vector.tensor_tensor(beat, other, mine, ALU.is_gt))
                done(nc.vector.tensor_tensor(beat, beat, same, ALU.add))
                done(nc.vector.tensor_reduce(rank[:, s], beat, AX_X, ALU.add))
            dve.wait_ge(*exp_ready.at(1))
            done(nc.vector.scalar_tensor_tensor(p, rank, 2.0, p, ALU.is_lt, ALU.mult))
            done(nc.vector.tensor_reduce(total, p, AX_X, ALU.add))
            done(nc.vector.reciprocal(total, total))
            done(nc.vector.tensor_tensor(gates, p, along(total, EXPERTS), ALU.mult))

        @block.scalar
        def _(act):
            act.wait_ge(*shifted.at(1))
            nc.scalar.activation(p, p, ACT.Exp).then_inc(exp_ready.up(1), 1)


def spread_gates(core, gates, shares):
    nc = core.nc
    diag_ready, spread, copied = (core.counted(s) for s in ("diag_ready", "spread", "copied"))
    diag = core.take(2, 2, P)
    with nc.Block(no_gpsimd_drain=True) as block:
        @block.vector
        def _(dve):
            for e in range(EXPERTS):
                if e >= 2:
                    dve.wait_ge(*spread.at(e - 1))
                for s in range(2):
                    ins = nc.vector.tensor_scalar(diag[:, e % 2, s], core.const("ident"), gates[:, s, e:e + 1], None, ALU.mult)
                ins.then_inc(diag_ready.up(1), 1)

        @block.tensor
        def _(pe):
            for e in range(EXPERTS):
                pe.wait_ge(*diag_ready.at(e + 1))
                if e >= 4:
                    pe.wait_ge(*copied.at(e - 3))
                nc.tensor.matmul(core.ps[:, e % 4, 0:T], core.const("ones"), diag[:, e % 2].rearrange("p a b -> p (a b)"),
                                 start=True, stop=True).then_inc(spread.up(1), 1)

        @block.scalar
        def _(act):
            for e in range(EXPERTS):
                act.wait_ge(*spread.at(e + 1))
                nc.scalar.activation(shares[:, e], core.ps[:, e % 4, 0:T], ACT.Copy).then_inc(copied.up(1), 1)


def second_block(core, x, mods, consts2):
    nc = core.nc
    base = core.at
    band = consts2[:, 0:8 * T].rearrange("p (g s t) -> p g s t", g=4, s=2)
    dist = consts2[:, 8 * T:10 * T].rearrange("p (a b) -> p a b", a=2)
    earlier = consts2[:, 10 * T:].rearrange("p (a b) -> p a b", a=EXPERTS)
    h, sq, stat = core.take(KT, T), core.take(KT, T), core.take(T)
    act_buf = core.take(2, T)
    mark = core.at

    modulate(core, "even", x, h, mods[0], 8, 0)
    prow, qt, kt, vrow, mix = core.take(2, 512), core.take(4, T), core.take(2, T), core.take(2, P), core.take(KT, T)
    pooled = core.take(4, T)
    even_inputs(core, h, prow, qt, kt, vrow)
    pooling(core, prow, band, pooled, mix)
    attention(core, qt, kt, vrow, dist, mix)
    project(core, "even_out", mix, D, residual(core, x, mods[0], 16))
    layer_norm(core, "ln00", x, 0, sq, stat)
    core.at = mark
    modulate(core, "swiglu_in", x, h, mods[0], 32, 24)
    ffn(core, "swiglu", h, groups(FFN), act_buf, residual(core, x, mods[0], 40))
    layer_norm(core, "ln01", x, 1, sq, stat)

    modulate(core, "odd", x, h, mods[1], 8, 0)
    u, v, vr = core.take(KT, T), core.take(KT, T), core.take(SG_GROUPS, 2, P)
    project(core, "odd_in", h, 2 * D, lambda act, f, sums: nc.scalar.activation(
        (u if f < KT else v)[:, f % KT], sums, ACT.Gelu_apprx_tanh), on="scalar")
    column_norm(core, "sg_norm", v, v, sq, stat, LN_EPS, lambda k: [
        (slice(0, T), core.col("sg_g")[:, k:k + 1], core.col("sg_b")[:, k:k + 1])], True)
    spatial_gate(core, u, v, vr)
    project(core, "odd_out", u, D, residual(core, x, mods[1], 16))
    layer_norm(core, "ln10", x, 2, sq, stat)
    core.at = mark
    modulate(core, "moe_in", x, h, mods[1], 32, 24)
    gates, shares = core.take(2, EXPERTS), core.take(EXPERTS, T)
    route(core, h, earlier, gates)
    spread_gates(core, gates, shares)
    plan = [(e * EXPERT_FFN + c, n) for e in range(EXPERTS) for c, n in groups(EXPERT_FFN)]
    ffn(core, "moe", h, plan, act_buf, residual(core, x, mods[1], 40), gates=lambda f: shares[:, f * P // EXPERT_FFN])
    layer_norm(core, "ln11", x, 3, sq, stat)
    core.at = base


def program(nc, tokens, params, params2, consts, consts2, weights, out):
    with ExitStack() as ctx:
        core = Core(nc, ctx, weights, stream_plan())
        x = core.take(KT, T)
        cond = core.take(KT, 3)
        mod, *mods = core.take(48, 2), core.take(48, 1), core.take(48, 1)
        mark = core.at
        core.cols, core.cols_of = core.take(N_COLS), COLS
        hall = core.arena[:, 32512 - KT * TALL:32512].rearrange("p (k t) -> p k t", k=KT)
        load_inputs(core, [(core.cols, params), (core.consts, consts), (hall, tokens), (x, tokens[:, :, TC:TALL]),
                           (core.arena[:, 16000:16096], params2[:, COLS_2["ada_b"]])])
        silu_done = core.counted("cond_silu_done")
        with nc.Block(no_gpsimd_drain=True) as block:
            @block.scalar
            def _(act):
                nc.scalar.activation(cond, core.col("cond", KT, 3), ACT.Silu).then_inc(silu_done.up(1), 1)
        conditioning(core, "mod", cond, 2, core.col("b_mod"), mod)
        for l in range(DEPTH_2):
            conditioning(core, f"ada{l}", cond[:, :, 2:3], 1, core.arena[:, 16000 + 48 * l:16048 + 48 * l], mods[l])
        first_block(core, x, hall, mod, cond)
        core.at = mark
        core.cols, core.cols_of = core.take(N_COLS_2), COLS_2
        c2 = core.take(N_CONSTS_2)
        landed = core.sem("inputs2_landed")
        with nc.Block(no_gpsimd_drain=True) as block:
            @block.scalar
            def _(act):
                act.dma_start(core.cols, params2).then_inc(landed, 16)
                act.dma_start(c2, consts2).then_inc(landed, 16)
                act.wait_ge(landed, 32)
        second_block(core, x, mods, c2)
        stored = core.sem("out_stored")
        with nc.Block(no_gpsimd_drain=True) as block:
            @block.sync
            def _(sp):
                sp.dma_start(out, x).then_inc(stored, 16)
                sp.wait_ge(stored, 16)



def columns(a):
    a = np.ascontiguousarray(a)
    return a.reshape(-1, P).T


def rows_tile(w):
    return w.reshape(w.shape[0] // P, P, w.shape[1]).transpose(1, 0, 2).reshape(P, -1)


def everywhere(a):
    return np.broadcast_to(np.asarray(a).reshape(1, -1), (P, np.asarray(a).size))


def kernel(**inputs):
    import concourse.bacc as bacc
    from concourse.bass_utils import run_bass_kernel_spmd as run

    a = {k: np.asarray(v) for k, v in inputs.items()}
    cond = np.stack([a["c"][0], a["c_ctx"], a["c_2"][0]], axis=-1)
    pieces = dict(cond=rows_tile(cond), b_mod=columns(a["b_mod"]), norm1_g=columns(a["norm1_g"]), norm2_g=columns(a["norm2_g"]),
                  final_g=columns(a["final_norm_g"]), conv_w=columns(a["gdn_conv_w"]), ffn_conv_w=columns(a["ffn_conv_w"]),
                  ffn_conv_b=columns(a["ffn_conv_b"]), gdn_norm_g=columns(a["gdn_norm_g"]), a_log=everywhere(a["gdn_a_log"]),
                  dt_bias=everywhere(a["gdn_dt_bias"]), w_ba=rows_tile(a["gdn_w_in"][0][:, 4 * D:]))
    params = np.concatenate([pieces[k] for k in PARAMS_1], axis=1)
    kv = a["ev_w_in_2"][0][:, D:]
    pieces = dict(ada_b=columns(a["ada_b_2"]), ln_g=columns(a["ln_g_2"]), ln_b=columns(a["ln_b_2"]), pool_scale=columns(a["ev_pool_scale_2"]),
                  sink=everywhere(a["ev_sink_2"]), sg_g=columns(a["od_sg_ln_g_2"]), sg_b=columns(a["od_sg_ln_b_2"]),
                  b_s=everywhere(a["od_b_s_2"]), w_s=a["od_w_s_2"][0].transpose(2, 0, 1).reshape(P, -1),
                  pool_w=a["ev_pool_w_2"][0].transpose(1, 0, 2).reshape(P, -1), w_router=rows_tile(a["moe_w_router_2"][0]))
    params2 = np.concatenate([pieces[k] for k in PARAMS_2], axis=1)
    tokens = np.concatenate([a["ctx"][0], a["x"][0]]).T
    tokens = rows_tile(tokens).reshape(P, KT, TALL)
    tiles = []

    def stream(block):
        t = np.zeros((P, TILE), np.float32)
        t[:, :block.shape[1]] = block
        tiles.append(t)

    def stream_columns(w):
        for c, n in groups(w.shape[1]):
            stream(rows_tile(w[:, c:c + n]))

    def stream_ffn(first, second, down):
        for c, n in groups(first.shape[1]):
            stream(rows_tile(first[:, c:c + n]))
            stream(rows_tile(second[:, c:c + n]))
            stream(rows_tile(down[c:c + n]))

    stream_columns(a["w_mod"][0])
    stream_columns(a["ada_w_2"][0])
    stream_columns(a["ada_w_2"][1])
    stream_columns(a["gdn_w_in"][0][:, :4 * D])
    stream_columns(a["gdn_w_out"][0])
    stream_ffn(a["ffn_w_in"][0][:, :FFN], a["ffn_w_in"][0][:, FFN:], a["ffn_w_out"][0])
    stream_columns(a["ev_w_in_2"][0][:, :D])
    stream(rows_tile(np.concatenate([kv[:, 0:64], kv[:, 0:64], kv[:, 64:128], kv[:, 64:128], kv[:, 128:256]], axis=1)))
    stream_columns(a["ev_w_out_2"][0])
    stream_ffn(a["ffn_w_gate_2"][0], a["ffn_w_up_2"][0], a["ffn_w_down_2"][0])
    stream_columns(a["od_w_in_2"][0])
    stream_columns(a["od_w_out_2"][0])
    for e in range(EXPERTS):
        stream_ffn(a["moe_w_gate_2"][0, e], a["moe_w_up_2"][0, e], a["moe_w_down_2"][0, e])
    sent = dict(tokens=tokens, params=params, params2=params2, consts=constants(), consts2=constants_2(), weights=np.stack(tiles))
    nc = bacc.Bacc("TRN2", target_bir_lowering=False, num_devices=1)
    sent = {k: np.ascontiguousarray(v) for k, v in sent.items()}
    aps = [nc.dram_tensor(k, v.shape, F32, kind="ExternalInput").ap() for k, v in sent.items()]
    out = nc.dram_tensor("out", (P, KT, T), F32, kind="ExternalOutput").ap()
    program(nc, *aps, out)
    r = run(nc, [sent], core_ids=[0])
    got = r.results[0]["out"]
    return np.ascontiguousarray(got.transpose(2, 1, 0).reshape(1, T, D))
```

```python
from contextlib import ExitStack

import numpy as np

import concourse.bass as bass
from concourse import mybir

F32 = mybir.dt.float32
I32 = mybir.dt.int32
ALU = mybir.AluOpType
ACT = mybir.ActivationFunctionType
AX_X = mybir.AxisListType.X

P = 128
D = 1024
KT = D // P
T = 256
TC = 256
TALL = TC + T
EPS = 1e-6
LN_EPS = 1e-5

TILE = 4096
GROUP = TILE // KT
DOWN_ROWS = TILE // D
RING = 5

HEADS = 8
GDN_CONV = 5
CHUNKS = TALL // P
LAT0 = TC // P
LEVELS = (2, 4, 8, 16, 32, 64)
FFN = 2816
FT = FFN // P
FFN_CONV = 3

DEPTH_2 = 2
ALPHA = (2.0 * DEPTH_2) ** 0.25
WINDOWS = (2, 4, 8, 16)
Q_HEADS = 8
HEAD = 64
KV_HEADS = 2
SLOPES = [2.0 ** (-8.0 * (h + 1) / Q_HEADS) for h in range(Q_HEADS)]
WINDOW = 128
FAR = 1e33
SG_GROUPS = 8
EXPERTS = 8
EXPERT_FFN = 3584
EXPERT_TILES = 3 * EXPERT_FFN // GROUP
SLOTS = 128
MOE_RING = 7



PARAMS_1 = dict(cond=KT * 3, b_mod=48, norm1_g=KT, norm2_g=KT, final_g=KT, conv_w=GDN_CONV * 24, ffn_conv_w=FFN_CONV * FT,
                ffn_conv_b=FT, gdn_norm_g=1, a_log=16, dt_bias=16, w_ba=KT * 32)


def offsets(sizes):
    at, out = 0, {}
    for name, n in sizes.items():
        out[name] = slice(at, at + n)
        at += n
    return out, at


PARAMS_2 = dict(ada_b=2 * 48, ln_g=4 * KT, ln_b=4 * KT, pool_scale=4, sink=Q_HEADS, sg_g=KT, sg_b=KT, b_s=SG_GROUPS * P,
                w_s=SG_GROUPS * P, pool_w=4 * P, w_router=KT * EXPERTS)
COLS, N_COLS = offsets(PARAMS_1)
COLS_2, N_COLS_2 = offsets(PARAMS_2)

CONSTS = dict(ident=P, ones=P, incl0=P, incl1=P, strict0=P, strict1=P,
              **{f"merge{s}_{d}": P for s in (1,) + LEVELS for d in range(2)})
CCOLS, N_CONSTS = offsets(CONSTS)
N_CONSTS_2 = 4 * 2 * T + 2 * T + EXPERTS * EXPERTS + SLOTS


def constants_2():
    s, t = np.arange(T)[:, None], np.arange(T)[None, :]
    parts = []
    for w in WINDOWS:
        lo, hi = np.maximum(t - w // 2, 0), np.minimum(t + w // 2 + 1, T)
        band = ((s >= lo) & (s < hi)) / (hi - lo) - (s == t)
        parts.append(rows_tile(band))
    dist = np.abs(s - t).astype(np.float64)
    parts.append(rows_tile(np.where(dist <= WINDOW, dist, FAR)))
    e = np.arange(EXPERTS)
    parts.append(np.broadcast_to((e[None, :] < e[:, None]).reshape(1, -1), (P, EXPERTS * EXPERTS)))
    parts.append(np.broadcast_to(np.arange(SLOTS).reshape(1, -1), (P, SLOTS)))
    assert 2 * SLOTS >= T
    return np.concatenate(parts, axis=1).astype(np.float32)


def constants():
    i, j = np.arange(P)[:, None], np.arange(P)[None, :]
    m = dict(ident=i == j, ones=i == i + 0 * j, incl0=i >= j, incl1=i <= j, strict0=i > j, strict1=i < j)
    for s in (1,) + LEVELS:
        low = (i // (2 * s) == j // (2 * s)) & (i // s > j // s)
        m[f"merge{s}_0"], m[f"merge{s}_1"] = low, low.T
    return np.concatenate([np.broadcast_to(m[k], (P, P)) for k in CONSTS], axis=1).astype(np.float32)


def groups(width):
    return [(c, min(GROUP, width - c)) for c in range(0, width, GROUP)]



def column_tiles(width):
    return [n * KT for _, n in groups(width)]


def ffn_tiles(width):
    out = []
    for _, n in groups(width):
        out += [n * KT, n * KT, n // P * D]
    return out


def stream_plan():
    return (column_tiles(6 * D) + column_tiles(4 * D) + column_tiles(6 * D) * DEPTH_2 + column_tiles(D) + ffn_tiles(FFN)
            + column_tiles(D) + [3 * P * KT] + column_tiles(D) + ffn_tiles(FFN)
            + column_tiles(2 * D) + column_tiles(D) + ffn_tiles(EXPERT_FFN) * EXPERTS)


class WeightStream:

    def __init__(self, plan, ring, dram, tile_loaded, tile_used):
        self.plan, self.ring, self.dram, self.tile_loaded, self.tile_used = plan, ring, dram, tile_loaded, tile_used
        self.issued = 0
        self.taken = 0
        self.due = 0

    def issue(self, sp, upto):
        while self.issued < min(upto, len(self.plan)):
            n = self.issued
            if n >= RING:
                sp.wait_ge(self.tile_used, n - RING + 1)
            words = self.plan[n]
            sp.dma_start(self.ring[:, n % RING, 0:words], self.dram[n, :, 0:words]).then_inc(self.tile_loaded[n % RING], 16)
            self.issued += 1

    def take(self, pe):
        n = self.taken
        pe.wait_ge(self.tile_loaded[n % RING], 16 * (n // RING + 1))
        self.taken += 1
        return self.ring[:, n % RING, :]


    def release(self, n=1):
        self.due += n

    def tell(self, mm):
        if self.due:
            mm.then_inc(self.tile_used, self.due)
            self.due = 0


class Counted:

    def __init__(self, sem):
        self.sem, self.base, self.told = sem, 0, 0

    def at(self, n):
        return self.sem, self.base + n

    def up(self, n):
        self.told += n
        return self.sem


class Chain:

    def __init__(self, eng, steps):
        self.eng, self.steps, self.n = eng, steps, 0

    def __call__(self, ins):
        self.n += 1
        ins.then_inc(self.steps.up(1), 1)
        self.eng.wait_ge(*self.steps.at(self.n))



class Core:

    def __init__(self, nc, ctx, weights, plan):
        self.nc, self.ctx, self.counts = nc, ctx, {}
        self.arena = ctx.enter_context(nc.sbuf_tensor("arena", [P, 32512], F32))
        self.ps = ctx.enter_context(nc.psum_tensor("ps", [P, 8, 512], F32))
        ring = ctx.enter_context(nc.sbuf_tensor("ring", [P, RING, TILE], F32))
        self.w = WeightStream(plan, ring, weights, [self.sem(f"tile_loaded{i}") for i in range(RING)], self.sem("tile_used"))
        self.at = 0
        self.consts = self.take(N_CONSTS)

    def sem(self, name):
        return self.ctx.enter_context(self.nc.semaphore(name))

    def counted(self, name):
        s = self.counts.setdefault(name, None) or Counted(self.sem(name))
        self.counts[name] = s
        s.base, s.told = s.base + s.told, 0
        return s

    def take(self, *shape):
        n = int(np.prod(shape))
        a = self.arena[:, self.at:self.at + n]
        self.at += n
        assert self.at <= 32512, self.at
        if len(shape) == 2:
            a = a.rearrange("p (a b) -> p a b", a=shape[0])
        if len(shape) == 3:
            a = a.rearrange("p (a b c) -> p a b c", a=shape[0], b=shape[1])
        if len(shape) == 4:
            a = a.rearrange("p (a b c d) -> p a b c d", a=shape[0], b=shape[1], c=shape[2])
        return a

    def const(self, name):
        return self.consts[:, CCOLS[name]]

    def col(self, name, *shape):
        a = self.cols[:, self.cols_of[name]]
        if len(shape) == 2:
            a = a.rearrange("p (a b) -> p a b", a=shape[0])
        return a


def over(ap, n):
    return ap.unsqueeze(1).to_broadcast([P, n, ap.shape[1]])


def along(ap, n):
    return ap.unsqueeze(2).to_broadcast([P, ap.shape[1], n])


def load_inputs(core, loads):
    nc = core.nc
    landed = core.sem("inputs_landed")
    with nc.Block(no_gpsimd_drain=True) as block:
        @block.sync
        def _(sp):
            core.w.issue(sp, RING)

        @block.scalar
        def _(act):
            for dst, src in loads:
                act.dma_start(dst, src).then_inc(landed, 16)
            act.wait_ge(landed, 16 * len(loads))


CONDS = 3
MOD_TILES = 6 * D // GROUP


def condition_rows(core, pe, cond, rows):
    tile = core.w.take(pe).rearrange("p (k c) -> p k c", k=KT)
    for k in range(KT):
        mm = core.nc.tensor.matmul(rows, cond[:, k], tile[:, k], start=(k == 0), stop=(k == KT - 1))
        if k == 0:
            core.w.tell(mm)
    core.w.release()
    return mm


def condition_columns(core, rows, columns):
    for j in range(GROUP // P):
        tr = core.nc.tensor.transpose(columns[:, j * CONDS:(j + 1) * CONDS], rows[:, j * P:(j + 1) * P], core.const("ident")[0:CONDS, 0:CONDS])
    return tr


def conditioning(core, cond, bias, mod):
    nc, w = core.nc, core.w
    rows_ready, rows_copied, columns_ready, chain = (core.counted(s) for s in ("mod_rows", "mod_rows_sb", "mod_columns", "chain"))
    at = core.at
    buf = core.take(2, GROUP)
    core.at = at
    with nc.Block(no_gpsimd_drain=True) as block:
        @block.sync
        def _(sp):
            w.issue(sp, w.taken + MOD_TILES + RING)

        @block.tensor
        def _(pe):
            for g in range(MOD_TILES + 1):
                if g < MOD_TILES:
                    if g >= 2:
                        pe.wait_ge(*rows_copied.at(g - 1))
                    condition_rows(core, pe, cond, core.ps[0:CONDS, g % 2]).then_inc(rows_ready.up(1), 1)
                if g:
                    pe.wait_ge(*rows_copied.at(g))
                    tr = condition_columns(core, buf[0:CONDS, (g - 1) % 2], core.ps[:, 2, 4 * CONDS * (g - 1):4 * CONDS * g])
            tr.then_inc(columns_ready.up(1), 1)
            pe.wait_ge(*columns_ready.at(1))
            w.tell(pe.nop())

        @block.scalar
        def _(act):
            for g in range(MOD_TILES):
                act.wait_ge(*rows_ready.at(g + 1))
                nc.scalar.activation(buf[0:CONDS, g % 2], core.ps[0:CONDS, g % 2], ACT.Copy).then_inc(rows_copied.up(1), 1)

        @block.vector
        def _(dve):
            dve.wait_ge(*columns_ready.at(1))
            nc.vector.tensor_tensor(mod, core.ps[:, 2, 0:48 * CONDS].rearrange("p (f r) -> p f r", r=CONDS)[:, :, 0:2],
                                    along(bias, 2), ALU.add).then_inc(chain.up(1), 1)


def column_norm(core, name, src, dst, sq, stat, eps, affine, centred):
    nc = core.nc
    n = src.shape[2]
    squares_ready, sums_ready, mean_ready, centred_ready, var_ready, root_ready, chain = (
        core.counted(s) for s in ("squares_ready", "sums_ready", "mean_ready", "centred_ready", "var_ready", "root_ready", "chain"))
    body = dst if centred else src
    with nc.Block(no_gpsimd_drain=True) as block:
        @block.tensor
        def _(pe):
            if centred:
                for k in range(KT):
                    mm = nc.tensor.matmul(core.ps[:, 0, 0:n], core.const("ones"), src[:, k], start=(k == 0), stop=(k == KT - 1))
                mm.then_inc(mean_ready.up(1), 1)
            for k in range(KT):
                pe.wait_ge(*squares_ready.at(k + 1))
                mm = nc.tensor.matmul(core.ps[:, 1, 0:n], core.const("ones"), sq[:, k], start=(k == 0), stop=(k == KT - 1))
            mm.then_inc(sums_ready.up(1), 1)

        @block.scalar
        def _(act):
            for k in range(KT):
                if centred:
                    act.wait_ge(*centred_ready.at(k + 1))
                nc.scalar.activation(sq[:, k], body[:, k], ACT.Square).then_inc(squares_ready.up(1), 1)
            act.wait_ge(*var_ready.at(1))
            nc.scalar.activation(stat, stat, ACT.Sqrt).then_inc(root_ready.up(1), 1)

        @block.vector
        def _(dve):
            done = Chain(dve, chain)
            if centred:
                dve.wait_ge(*mean_ready.at(1))
                done(nc.vector.tensor_scalar(stat, core.ps[:, 0, 0:n], 1.0 / D, None, ALU.mult))
                for k in range(KT):
                    nc.vector.tensor_tensor(dst[:, k], src[:, k], stat, ALU.subtract).then_inc(centred_ready.up(1), 1)
            dve.wait_ge(*sums_ready.at(1))
            nc.vector.tensor_scalar(stat, core.ps[:, 1, 0:n], 1.0 / D, eps, ALU.mult, ALU.add).then_inc(var_ready.up(1), 1)
            dve.wait_ge(*root_ready.at(1))
            done(nc.vector.reciprocal(stat, stat))
            if centred:
                dve.wait_ge(*centred_ready.at(KT))
            for k in range(KT):
                done(nc.vector.tensor_tensor(dst[:, k], body[:, k], stat, ALU.mult))
            for k in range(KT):
                for tokens, scale, shift in affine(k):
                    x = dst[:, k, tokens]
                    if shift is None:
                        ins = nc.vector.tensor_scalar(x, x, scale, None, ALU.mult)
                    else:
                        ins = nc.vector.tensor_scalar(x, x, scale, shift, ALU.mult, ALU.add)
                    ins.then_inc(chain.up(1), 1)


def project(core, name, rhs, width, finish, banks=4, on="vector"):
    nc, w = core.nc, core.w
    sums_ready, sums_used = core.counted("sums_ready"), core.counted("sums_used")
    n = rhs.shape[2]
    with nc.Block(no_gpsimd_drain=True) as block:
        @block.sync
        def _(sp):
            w.issue(sp, w.taken + len(groups(width)) + RING)

        @block.tensor
        def _(pe):
            for c, cols in groups(width):
                tile = w.take(pe)[:, 0:KT * cols].rearrange("p (k c) -> p k c", k=KT)
                for f in range(c // P, (c + cols) // P):
                    if f >= banks:
                        pe.wait_ge(*sums_used.at(f - banks + 1))
                    for k in range(KT):
                        mm = nc.tensor.matmul(core.ps[:, f % banks, 0:n], tile[:, k, f * P - c:f * P - c + P], rhs[:, k],
                                              start=(k == 0), stop=(k == KT - 1))
                        if k == 0:
                            w.tell(mm)
                    mm.then_inc(sums_ready.up(1), 1)
                w.release()
            pe.wait_ge(*sums_ready.at(width // P))
            w.tell(pe.nop())

        @(block.vector if on == "vector" else block.scalar)
        def _(eng):
            for f in range(width // P):
                eng.wait_ge(*sums_ready.at(f + 1))
                finish(eng, f, core.ps[:, f % banks, 0:n]).then_inc(sums_used.up(1), 1)


def gdn_project(core, h, q, k, v, gate, gates, pad, taps):
    nc, w = core.nc, core.w
    sums_ready, sums_used, pad_zero, padded, pad_used, conved, conv_used, gates_ready, chain = (
        core.counted(s) for s in ("sums_ready", "sums_used", "pad_zero", "padded", "pad_used", "conved", "conv_used", "gates_ready", "chain"))
    conv_w = core.col("conv_w", GDN_CONV, 24)
    w_ba = core.col("w_ba", KT, 32)

    def segments(f):
        return (1,) if f < HEADS or f >= 3 * HEADS else (0, 1)

    with nc.Block(no_gpsimd_drain=True) as block:
        @block.sync
        def _(sp):
            w.issue(sp, w.taken + 8 + RING)

        @block.tensor
        def _(pe):
            for g in range(8):
                tile = w.take(pe).rearrange("p (k c) -> p k c", k=KT)
                for f in range(4 * g, 4 * g + 4):
                    if f >= 4:
                        pe.wait_ge(*sums_used.at(f - 3))
                    first = TC * segments(f)[0]
                    for kk in range(KT):
                        mm = nc.tensor.matmul(core.ps[:, f % 4, first:TALL], tile[:, kk, (f % 4) * P:(f % 4 + 1) * P],
                                              h[:, kk, first:TALL], start=(kk == 0), stop=(kk == KT - 1))
                        if kk == 0:
                            w.tell(mm)
                    mm.then_inc(sums_ready.up(1), 1)
                w.release()
            for c in range(CHUNKS):
                for kk in range(KT):
                    mm = nc.tensor.matmul(core.ps[:, 4, c * 32:(c + 1) * 32], h[:, kk, c * P:(c + 1) * P], w_ba[:, kk],
                                          start=(kk == 0), stop=(kk == KT - 1))
                    if kk == 0:
                        w.tell(mm)
            mm.then_inc(gates_ready.up(1), 1)

        @block.scalar
        def _(act):
            act.wait_ge(*pad_zero.at(1))
            for f in range(33):
                if f < 32:
                    act.wait_ge(*sums_ready.at(f + 1))
                if f < 24:
                    if f >= 4:
                        act.wait_ge(*pad_used.at(f - 3))
                    for s in segments(f):
                        ins = nc.scalar.activation(pad[:, f % 4, s, 2:2 + T], core.ps[:, f % 4, s * T:(s + 1) * T], ACT.Copy)
                    ins.then_inc(padded.up(1), 1)
                    act.wait_ge(*padded.at(f + 1))
                    act.nop().then_inc(sums_used.up(1), 1)
                elif f < 32:
                    nc.scalar.activation(gate[:, f - 24], core.ps[:, f % 4, TC:TALL], ACT.Silu).then_inc(sums_used.up(1), 1)
                if 1 <= f < 25:
                    e = f - 1
                    act.wait_ge(*conved.at(e + 1))
                    dst = (q, k, v)[e // HEADS][:, e % HEADS]
                    for s in segments(e):
                        d = dst if e < HEADS else dst[:, s * T:(s + 1) * T]
                        ins = nc.scalar.activation(d, taps[:, e % 2, s], ACT.Silu)
                    ins.then_inc(conv_used.up(1), 1)

        @block.vector
        def _(dve):
            nc.vector.memset(pad, 0.0).then_inc(pad_zero.up(1), 1)
            done = Chain(dve, chain)
            for f in range(24):
                dve.wait_ge(*padded.at(f + 1))
                if f >= 2:
                    dve.wait_ge(*conv_used.at(f - 1))
                a, b = segments(f)[0], 2
                x, y = pad[:, f % 4, a:b], taps[:, f % 2, a:b]
                done(nc.vector.tensor_scalar(y, x[:, :, 0:T], conv_w[:, 0, f:f + 1], None, ALU.mult))
                for i in range(1, GDN_CONV):
                    ins = nc.vector.scalar_tensor_tensor(y, x[:, :, i:i + T], conv_w[:, i, f:f + 1], y, ALU.mult, ALU.add)
                    if i < GDN_CONV - 1:
                        done(ins)
                ins.then_inc(conved.up(1), 1)
                dve.wait_ge(*conved.at(f + 1))
                dve.nop().then_inc(pad_used.up(1), 1)
            dve.wait_ge(*gates_ready.at(1))
            nc.vector.tensor_copy(gates, core.ps[:, 4, 0:CHUNKS * 32].rearrange("p (c g) -> p c g", c=CHUNKS)).then_inc(chain.up(1), 1)


def gdn_gates(core, gates, beta, nbeta, kb_scale, kd_scale, alast, gc, g, tmp):
    nc = core.nc
    to_act, to_dve, sums_ready, g_ready, chain, achain = (core.counted(s) for s in ("to_act", "to_dve", "sums_ready", "g_ready", "chain", "achain"))
    raw = gates.rearrange("p c (d j h) -> p j d h c", d=2, j=2)
    z, e, r, ea = tmp
    n = HEADS * CHUNKS

    def flat(ap, d):
        return ap[:, d].rearrange("p h c -> p (h c)")

    with nc.Block(no_gpsimd_drain=True) as block:
        @block.vector
        def _(dve):
            done = Chain(dve, chain)
            dt = core.col("dt_bias", 2, HEADS)
            for d in range(2):
                done(nc.vector.tensor_tensor(z[:, d], raw[:, 1, d], along(dt[:, d], CHUNKS), ALU.add))
            done(nc.vector.tensor_scalar(r, z, 0.0, None, ALU.max))
            done(nc.vector.scalar_tensor_tensor(z, r, -2.0, z, ALU.mult, ALU.add))
            dve.nop().then_inc(to_act.up(1), 1)
            dve.wait_ge(*to_dve.at(1))
            done(nc.vector.tensor_tensor(r, r, e, ALU.add))
            for d in range(2):
                done(nc.vector.tensor_tensor(g[:, d], r[:, d], along(ea[:, d * HEADS:(d + 1) * HEADS], CHUNKS), ALU.mult))
            done(nc.vector.tensor_scalar(g, g, -1.0, None, ALU.mult))
            dve.nop().then_inc(g_ready.up(1), 1)
            dve.wait_ge(*sums_ready.at(1))
            for d in range(2):
                done(nc.vector.tensor_copy(flat(gc, d), core.ps[:, 0, d * n:(d + 1) * n]))
                done(nc.vector.tensor_copy(flat(alast, d), core.ps[:, 1, d * n:(d + 1) * n]))
            done(nc.vector.tensor_tensor(kd_scale, alast, gc, ALU.subtract))
            dve.nop().then_inc(to_act.up(1), 1)
            dve.wait_ge(*to_dve.at(2))
            done(nc.vector.tensor_tensor(kb_scale, kb_scale, beta, ALU.mult))
            done(nc.vector.tensor_scalar(nbeta, beta, -1.0, None, ALU.mult))

        @block.tensor
        def _(pe):
            pe.wait_ge(*g_ready.at(1))
            for d in range(2):
                nc.tensor.matmul(core.ps[:, 0, d * n:(d + 1) * n], core.const(f"incl{1 - d}"), flat(g, d), start=True, stop=True)
                mm = nc.tensor.matmul(core.ps[:, 1, d * n:(d + 1) * n], core.const("ones"), flat(g, d), start=True, stop=True)
            mm.then_inc(sums_ready.up(1), 1)

        @block.scalar
        def _(act):
            done = Chain(act, achain)
            for d in range(2):
                done(nc.scalar.activation(beta[:, d], raw[:, 0, d], ACT.Sigmoid))
            done(nc.scalar.activation(ea, core.col("a_log"), ACT.Exp))
            act.wait_ge(*to_act.at(1))
            done(nc.scalar.activation(e, z, ACT.Exp))
            done(nc.scalar.activation(e, e, ACT.Ln, bias=1.0))
            act.nop().then_inc(to_dve.up(1), 1)
            act.wait_ge(*to_act.at(2))
            done(nc.scalar.activation(kb_scale, gc, ACT.Exp))
            done(nc.scalar.activation(kd_scale, kd_scale, ACT.Exp))
            done(nc.scalar.activation(alast, alast, ACT.Exp))
            act.nop().then_inc(to_dve.up(1), 1)


def inverse_norms(core, name, x, out, sq, eps, div):
    nc = core.nc
    squares_ready, sums_ready, var_ready, root_ready, chain = (core.counted(s) for s in ("squares_ready", "sums_ready", "var_ready", "root_ready", "chain"))
    heads, n = x.shape[1], x.shape[2]
    with nc.Block(no_gpsimd_drain=True) as block:
        @block.tensor
        def _(pe):
            for h in range(heads):
                pe.wait_ge(*squares_ready.at(h + 1))
                if h >= 4:
                    pe.wait_ge(*var_ready.at(h - 3))
                nc.tensor.matmul(core.ps[:, h % 4, 0:n], core.const("ones"), sq[:, h % 2], start=True, stop=True).then_inc(sums_ready.up(1), 1)

        @block.scalar
        def _(act):
            for h in range(heads):
                if h >= 2:
                    act.wait_ge(*sums_ready.at(h - 1))
                nc.scalar.activation(sq[:, h % 2], x[:, h], ACT.Square).then_inc(squares_ready.up(1), 1)
            for h in range(heads):
                act.wait_ge(*var_ready.at(h + 1))
                nc.scalar.activation(out[:, h], out[:, h], ACT.Sqrt).then_inc(root_ready.up(1), 1)

        @block.vector
        def _(dve):
            for h in range(heads):
                dve.wait_ge(*sums_ready.at(h + 1))
                nc.vector.tensor_scalar(out[:, h], core.ps[:, h % 4, 0:n], 1.0 / div, eps, ALU.mult, ALU.add).then_inc(var_ready.up(1), 1)
            for h in range(heads):
                dve.wait_ge(*root_ready.at(h + 1))
                nc.vector.reciprocal(out[:, h], out[:, h]).then_inc(chain.up(1), 1)


def gdn_heads(core, cond, ada_b, mods, q, k, v, beta, nbeta, kb_scale, kd_scale, alast, gc, g, out, spare):
    nc, w = core.nc, core.w
    S = {s: core.counted(s) for s in (
        "start", "qkv", "rows", "k_rows", "bv", "kkqk", "tri_g", "gsum", "scaled", "edge", "decay", "lower", "lower_t", "lower_tsb",
        "seeds", "seeds_id", "t", "t_sb", "p", "merged", "wt", "wt_sb", "v", "v_sb", "ds", "state", "o", "qk_masked", "qk_t", "qk_tsb",
        "qd", "exp_g", "mod_rows", "mod_rows_sb", "mod_columns", "mod_added", "dve_chain", "act_chain", "pool_chain")}
    kh, vh, qh, kr = core.take(TALL), core.take(TALL), core.take(T), core.take(CHUNKS, P)
    bv, kb, kd = (core.take(2, CHUNKS, P) for _ in range(3))
    low, lowt, x, y = (spare[:, 2 * n:2 * n + 2].rearrange("p d (c n) -> p d c n", c=CHUNKS) for n in range(4))
    t, wt = core.take(2, CHUNKS, P), core.take(2, CHUNKS, P)
    tg, e = t, wt
    qkm, qkt, qd = (core.take(2, 2, P) for _ in range(3))
    vn, state = core.take(2, P), core.take(2, P)
    mod_row = core.take(GROUP)
    ps = core.ps

    def mod_step(h, n):
        if h == HEADS - 1 and n == NL - 1:
            return DEPTH_2 * MOD_TILES
        return 3 * h + n // 2 if n % 2 == 0 else None

    NL = len(LEVELS)
    order = ((0, 1, 2, 3), (1, 0, 3, 2))

    def bank(b):
        return ps[:, b].rearrange("p (c n) -> p c n", c=CHUNKS)

    with nc.Block(no_gpsimd_drain=True) as block:
        @block.sync
        def _(sp):
            w.issue(sp, w.taken + DEPTH_2 * MOD_TILES + RING)

        @block.tensor
        def _(pe):
            mm = nc.tensor.matmul
            for h in range(HEADS):
                pe.wait_ge(*S["qkv"].at(h + 1))
                for c in range(CHUNKS):
                    nc.tensor.transpose(bank(0)[:, c], kh[:, c * P:(c + 1) * P], core.const("ident"))
                for c in range(CHUNKS):
                    last = nc.tensor.transpose(bank(1)[:, c], vh[:, c * P:(c + 1) * P], core.const("ident"))
                last.then_inc(S["rows"].up(1), 1)
                for c in range(CHUNKS):
                    kc = kh[:, c * P:(c + 1) * P]
                    last = mm(bank(2)[:, c], kc, kc, start=True, stop=True)
                for c in range(2):
                    last = mm(bank(3)[:, c], qh[:, c * P:(c + 1) * P], kh[:, (LAT0 + c) * P:(LAT0 + c + 1) * P], start=True, stop=True)
                last.then_inc(S["kkqk"].up(1), 1)
                for d in range(2):
                    pe.wait_ge(*S["tri_g"].at(2 * h + d + 1))
                    mm(ps[:, 4 + d], core.const("ones"), tg[:, d].rearrange("p a b -> p (a b)"), start=True, stop=True).then_inc(S["gsum"].up(1), 1)
                for d in range(2):
                    pe.wait_ge(*S["qk_masked"].at(2 * h + d + 1))
                    for c in range(2):
                        last = nc.tensor.transpose(bank(6 + d)[:, c], qkm[:, d, c], core.const("ident"))
                    last.then_inc(S["qk_t"].up(1), 1)
                for d in range(2):
                    pe.wait_ge(*S["lower"].at(2 * h + d + 1))
                    if d == 0:
                        pe.wait_ge(*S["k_rows"].at(h + 1))
                        pe.wait_ge(*S["bv"].at(2 * h + 2))
                    for c in range(CHUNKS):
                        last = nc.tensor.transpose(bank(d)[:, c], low[:, d, c], core.const("ident"))
                    last.then_inc(S["lower_t"].up(1), 1)
                for n in range(NL):
                    for d in range(2):
                        pe.wait_ge(*S["seeds"].at(2 * h + d + 1))
                        if n:
                            pe.wait_ge(*S["merged"].at(2 * NL * h + 2 * (n - 1) + d + 1))
                        for c in range(CHUNKS):
                            last = mm(bank(2 + d)[:, c], lowt[:, d, c], x[:, d, c], start=True, stop=True)
                        last.then_inc(S["t"].up(1), 1)
                    u = mod_step(h, n)
                    if u is not None:
                        if n == 0:
                            pe.wait_ge(*S["qk_tsb"].at(2 * h + 2))
                        if u:
                            pe.wait_ge(*S["mod_rows_sb"].at(u))
                            if u >= 2:
                                pe.wait_ge(*S["mod_added"].at(u - 1))
                            condition_columns(core, mod_row[0:CONDS], ps[:, 7, 0:4 * CONDS]).then_inc(S["mod_columns"].up(1), 1)
                        if u < DEPTH_2 * MOD_TILES:
                            condition_rows(core, pe, cond, ps[0:CONDS, 6]).then_inc(S["mod_rows"].up(1), 1)
                    for d in range(2):
                        pe.wait_ge(*S["t_sb"].at(2 * NL * h + 2 * n + d + 1))
                        for c in range(CHUNKS):
                            if n < NL - 1:
                                w.tell(mm(bank(4 + d)[:, c], y[:, d, c], t[:, d, c], start=True, stop=True))
                        for c in range(CHUNKS):
                            last = mm(bank(d)[:, c], t[:, d, c], y[:, d, c], start=True, stop=True)
                        last.then_inc(S["p"].up(1), 1)
                pe.wait_ge(*S["scaled"].at(4 * h + 4))
                for d in range(2):
                    pe.wait_ge(*S["merged"].at(2 * NL * h + 2 * (NL - 1) + d + 1))
                    for c in range(CHUNKS):
                        last = mm(bank(2 + d)[:, c], kb[:, d, c], y[:, d, c], start=True, stop=True)
                    last.then_inc(S["wt"].up(1), 1)
                for n in range(CHUNKS):
                    for d in range(2):
                        c = order[d][n]
                        if n == 0:
                            pe.wait_ge(*S["merged"].at(2 * NL * (h + 1)))
                        last = mm(bank(d)[:, n], y[:, d, c], bv[:, d, c], start=True, stop=(n == 0))
                        if n:
                            pe.wait_ge(*S["wt_sb"].at(2 * h + d + 1))
                            pe.wait_ge(*S["state"].at(6 * h + 2 * (n - 1) + d + 1))
                            last = mm(bank(d)[:, n], wt[:, d, c], state[:, d], start=False, stop=True)
                        last.then_inc(S["v"].up(1), 1)
                    for d in range(2):
                        c = order[d][n]
                        if c >= LAT0:
                            if n == LAT0:
                                done = min(3 * h + 3, DEPTH_2 * MOD_TILES)
                                pe.wait_ge(*S["mod_rows_sb"].at(done))
                                pe.wait_ge(*S["mod_added"].at(done - 1 + (h == HEADS - 1)))
                                pe.wait_ge(*S["qk_tsb"].at(2 * h + 2))
                                pe.wait_ge(*S["qd"].at(2 * h + 2))
                            mm(bank(6 + d)[:, c - LAT0], state[:, d], qd[:, d, c - LAT0], start=True, stop=False)
                        pe.wait_ge(*S["v_sb"].at(8 * h + 2 * n + d + 1))
                        if c >= LAT0:
                            mm(bank(6 + d)[:, c - LAT0], vn[:, d], qkt[:, d, c - LAT0], start=False, stop=True).then_inc(S["o"].up(1), 1)
                        if n < CHUNKS - 1:
                            mm(bank(4 + d)[:, n], kd[:, d, c], vn[:, d], start=True, stop=True).then_inc(S["ds"].up(1), 1)

        @block.scalar
        def _(act):
            done = Chain(act, S["act_chain"])
            for h in range(HEADS):
                act.wait_ge(*S["rows"].at(h + 1))
                nc.scalar.activation(kr, bank(0), ACT.Copy).then_inc(S["k_rows"].up(1), 1)
                for d in range(2):
                    act.wait_ge(*S["gsum"].at(2 * h + d + 1))
                    nc.scalar.activation(qd[:, d].rearrange("p a b -> p (a b)"), ps[:, 4 + d, TC:TALL], ACT.Exp).then_inc(S["exp_g"].up(1), 1)
                    act.wait_ge(*S["edge"].at(2 * h + d + 1))
                    nc.scalar.activation(e[:, d], e[:, d], ACT.Exp, scale=-1.0).then_inc(S["decay"].up(1), 1)
                for d in range(2):
                    act.wait_ge(*S["qk_t"].at(2 * h + d + 1))
                    nc.scalar.activation(qkt[:, d], bank(6 + d)[:, 0:2], ACT.Copy).then_inc(S["qk_tsb"].up(1), 1)
                for d in range(2):
                    act.wait_ge(*S["lower_t"].at(2 * h + d + 1))
                    nc.scalar.activation(lowt[:, d], bank(d), ACT.Copy).then_inc(S["lower_tsb"].up(1), 1)
                for n in range(NL):
                    for d in range(2):
                        act.wait_ge(*S["t"].at(2 * NL * h + 2 * n + d + 1))
                        nc.scalar.activation(t[:, d], bank(2 + d), ACT.Copy).then_inc(S["t_sb"].up(1), 1)
                    u = mod_step(h, n)
                    if u is not None and u < DEPTH_2 * MOD_TILES:
                        act.wait_ge(*S["mod_rows"].at(u + 1))
                        nc.scalar.activation(mod_row[0:CONDS], ps[0:CONDS, 6], ACT.Copy).then_inc(S["mod_rows_sb"].up(1), 1)
                for d in range(2):
                    act.wait_ge(*S["wt"].at(2 * h + d + 1))
                    nc.scalar.activation(wt[:, d], bank(2 + d), ACT.Copy, scale=-1.0).then_inc(S["wt_sb"].up(1), 1)
                for n in range(CHUNKS):
                    for d in range(2):
                        act.wait_ge(*S["v"].at(8 * h + 2 * n + d + 1))
                        if n:
                            act.wait_ge(*S["ds"].at(6 * h + 2 * (n - 1) + d + 1))
                        nc.scalar.activation(vn[:, d], bank(d)[:, n], ACT.Copy).then_inc(S["v_sb"].up(1), 1)

        @block.gpsimd
        def _(pool):
            for h in range(HEADS):
                if h:
                    pool.wait_ge(*S["start"].at(h))
                for d in range(2):
                    tri = over(core.const(f"incl{1 - d}"), CHUNKS)
                    nc.gpsimd.tensor_tensor(tg[:, d], tri, along(g[:, d, h], P), ALU.mult).then_inc(S["tri_g"].up(1), 1)
                for d in range(2):
                    nc.gpsimd.tensor_copy(x[:, d], over(core.const("ident"), CHUNKS)).then_inc(S["seeds_id"].up(1), 1)
                    nc.gpsimd.tensor_copy(y[:, d], over(core.const("ident"), CHUNKS)).then_inc(S["seeds_id"].up(1), 1)
                pool.wait_ge(*S["k_rows"].at(h + 1))
                for d in range(2):
                    nc.gpsimd.tensor_tensor(kb[:, d], kr, along(kb_scale[:, d, h], P), ALU.mult).then_inc(S["scaled"].up(1), 1)
                    nc.gpsimd.tensor_tensor(kd[:, d], kr, along(kd_scale[:, d, h], P), ALU.mult).then_inc(S["scaled"].up(1), 1)

        @block.vector
        def _(dve):
            done = Chain(dve, S["dve_chain"])

            def merge(dst, mask, src):
                return nc.vector.copy_predicated(dst, over(core.const(mask), CHUNKS).bitcast(I32), src)

            for h in range(HEADS):
                done(nc.vector.tensor_copy(kh, k[:, h]))
                done(nc.vector.tensor_copy(vh, v[:, h]))
                done(nc.vector.tensor_scalar(qh, q[:, h], float(P) ** -0.5, None, ALU.mult))
                dve.nop().then_inc(S["qkv"].up(1), 1)
                dve.wait_ge(*S["rows"].at(h + 1))
                for d in range(2):
                    dve.wait_ge(*S["rows"].at(h + 1))
                    nc.vector.tensor_tensor(bv[:, d], bank(1), along(beta[:, d, h], P), ALU.mult).then_inc(S["bv"].up(1), 1)
                for d in range(2):
                    dve.wait_ge(*S["exp_g"].at(2 * h + d + 1))
                    for c in range(CHUNKS):
                        ins = nc.vector.tensor_scalar(e[:, d, c], bank(4 + d)[:, c], gc[:, d, h, c:c + 1], 0.0, ALU.subtract, ALU.max)
                    ins.then_inc(S["edge"].up(1), 1)
                for d in range(2):
                    dve.wait_ge(*S["decay"].at(2 * h + d + 1))
                    done(nc.vector.tensor_tensor(e[:, d], e[:, d], over(core.const(f"incl{d}"), CHUNKS), ALU.mult))
                    dve.wait_ge(*S["kkqk"].at(h + 1))
                    nc.vector.tensor_tensor(qkm[:, d], bank(3)[:, 0:2], e[:, d, LAT0:CHUNKS], ALU.mult).then_inc(S["qk_masked"].up(1), 1)
                    for c in range(CHUNKS):
                        ins = nc.vector.scalar_tensor_tensor(low[:, d, c], bank(2)[:, c], nbeta[:, d, h, c:c + 1], e[:, d, c], ALU.mult, ALU.mult)
                    done(ins)
                    done(nc.vector.tensor_tensor(low[:, d], low[:, d], over(core.const(f"strict{d}"), CHUNKS), ALU.mult))
                    dve.nop().then_inc(S["lower"].up(1), 1)
                for d in range(2):
                    dve.wait_ge(*S["exp_g"].at(2 * h + d + 1))
                    nc.vector.tensor_tensor(qd[:, d].rearrange("p a b -> p (a b)"), qd[:, d].rearrange("p a b -> p (a b)"), qh, ALU.mult).then_inc(S["qd"].up(1), 1)
                dve.wait_ge(*S["seeds_id"].at(4 * h + 4))
                for d in range(2):
                    dve.wait_ge(*S["lower_tsb"].at(2 * h + d + 1))
                    done(merge(x[:, d], f"merge1_{d}", low[:, d]))
                    done(merge(y[:, d], f"merge1_{1 - d}", lowt[:, d]))
                    dve.nop().then_inc(S["seeds"].up(1), 1)
                for n, s in enumerate(LEVELS):
                    for d in range(2):
                        dve.wait_ge(*S["p"].at(2 * NL * h + 2 * n + d + 1))
                        if n < NL - 1:
                            done(merge(x[:, d], f"merge{s}_{d}", bank(4 + d)))
                        done(merge(y[:, d], f"merge{s}_{1 - d}", bank(d)))
                        dve.nop().then_inc(S["merged"].up(1), 1)
                    u = mod_step(h, n)
                    if u:
                        dve.wait_ge(*S["mod_columns"].at(u))
                        l, at = divmod(4 * (u - 1), 48)
                        nc.vector.tensor_tensor(mods[l][:, at:at + 4], ps[:, 7, 0:4 * CONDS].rearrange("p (f r) -> p f r", r=CONDS)[:, :, 2:3],
                                                ada_b[:, 48 * l + at:48 * l + at + 4].unsqueeze(2), ALU.add).then_inc(S["mod_added"].up(1), 1)
                for n in range(CHUNKS - 1):
                    for d in range(2):
                        c = order[d][n]
                        dve.wait_ge(*S["ds"].at(6 * h + 2 * n + d + 1))
                        if n == 0:
                            nc.vector.tensor_copy(state[:, d], bank(4 + d)[:, 0]).then_inc(S["state"].up(1), 1)
                        else:
                            if n == LAT0:
                                dve.wait_ge(*S["o"].at(4 * h + d + 1))
                            nc.vector.scalar_tensor_tensor(state[:, d], state[:, d], alast[:, d, h, c:c + 1], bank(4 + d)[:, n],
                                                           ALU.mult, ALU.add).then_inc(S["state"].up(1), 1)
                        dve.wait_ge(*S["state"].at(6 * h + 2 * n + d + 1))
                dve.wait_ge(*S["o"].at(4 * h + 4))
                o = out[:, h].rearrange("p (c n) -> p c n", c=2)
                done(nc.vector.tensor_copy(o, bank(6)[:, 0:2]))
                done(nc.vector.tensor_tensor(o, bank(7)[:, 0:2], o, ALU.add))
                dve.nop().then_inc(S["start"].up(1), 1)


def ffn(core, name, rhs, plan, act_buf, finish, conv=None, gates=None):
    nc, w = core.nc, core.w
    S = {s: core.counted(s) for s in ("up_ready", "up_used", "gated", "act_ready", "act_used", "pad_zero", "padded", "conved", "chain")}
    tiles = sum(n for _, n in plan) // P
    banks = 4

    def acc(m):
        return core.ps[:, 4 + m // 2, (m % 2) * T:(m % 2 + 1) * T]

    with nc.Block(no_gpsimd_drain=True) as block:
        @block.sync
        def _(sp):
            w.issue(sp, w.taken + 3 * len(plan) + RING)

        @block.tensor
        def _(pe):
            down_tiles = {}

            def up(f, first, second, j, last):
                if f >= banks:
                    pe.wait_ge(*S["act_ready"].at(f - banks + 1))
                for half, tile in ((0, first), (1, second)):
                    for k in range(KT):
                        mm = nc.tensor.matmul(core.ps[:, f % banks, half * T:(half + 1) * T], tile[:, k, j * P:(j + 1) * P], rhs[:, k],
                                              start=(k == 0), stop=(k == KT - 1))
                        if k == 0:
                            w.tell(mm)
                mm.then_inc(S["up_ready"].up(1), 1)
                if last:
                    w.release(2)

            def down(f):
                tile, j, last = down_tiles.pop(f)
                pe.wait_ge(*S["act_ready"].at(f + 1))
                for m in range(KT):
                    mm = nc.tensor.matmul(acc(m), tile[:, j, m * P:(m + 1) * P], act_buf[:, f % 2], start=(f == 0 and m % 2 == 0),
                                          stop=(f == tiles - 1), skip_group_check=True)
                    if m == 0:
                        w.tell(mm)
                mm.then_inc(S["act_used"].up(1), 1)
                if last:
                    w.release()

            for c, cols in plan:
                n = cols // P
                first = w.take(pe)[:, 0:KT * cols].rearrange("p (k c) -> p k c", k=KT)
                second = w.take(pe)[:, 0:KT * cols].rearrange("p (k c) -> p k c", k=KT)
                for j in range(n):
                    f = c // P + j
                    up(f, first, second, j, j == n - 1)
                    if f:
                        down(f - 1)
                    if j == 0:
                        third = w.take(pe)[:, 0:n * D].rearrange("p (j c) -> p j c", j=n)
                    down_tiles[f] = (third, j, j == n - 1)
            down(tiles - 1)
            pe.wait_ge(*S["act_used"].at(tiles))
            w.tell(pe.nop())

        @block.scalar
        def _(act):
            if conv:
                pad, taps, bias, cv = conv
                act.wait_ge(*S["pad_zero"].at(1))
            for f in range(tiles):
                act.wait_ge(*S["up_ready"].at(f + 1))
                if conv:
                    if f >= 2:
                        act.wait_ge(*S["conved"].at(f - 1))
                    nc.scalar.activation(pad[:, f % 2, 1:1 + T], core.ps[:, f % banks, T:2 * T], ACT.Copy).then_inc(S["padded"].up(1), 1)
                    act.wait_ge(*S["conved"].at(f + 1))
                    nc.scalar.activation(cv[:, f % 2], cv[:, f % 2], ACT.Silu).then_inc(S["gated"].up(1), 1)
                else:
                    if f >= 2:
                        act.wait_ge(*S["act_used"].at(f - 1))
                    nc.scalar.activation(act_buf[:, f % 2], core.ps[:, f % banks, 0:T], ACT.Silu).then_inc(S["gated"].up(1), 1)

        @block.vector
        def _(dve):
            done = Chain(dve, S["chain"])
            if conv:
                nc.vector.memset(conv[0], 0.0).then_inc(S["pad_zero"].up(1), 1)
            for f in range(tiles):
                buf = act_buf[:, f % 2]
                if conv:
                    pad, taps, bias, cv = conv
                    dve.wait_ge(*S["padded"].at(f + 1))
                    y = cv[:, f % 2]
                    done(nc.vector.tensor_scalar(y, pad[:, f % 2, 0:T], taps[:, 0, f:f + 1], bias[:, f:f + 1], ALU.mult, ALU.add))
                    done(nc.vector.scalar_tensor_tensor(y, pad[:, f % 2, 1:1 + T], taps[:, 1, f:f + 1], y, ALU.mult, ALU.add))
                    nc.vector.scalar_tensor_tensor(y, pad[:, f % 2, 2:2 + T], taps[:, 2, f:f + 1], y, ALU.mult, ALU.add).then_inc(S["conved"].up(1), 1)
                    dve.wait_ge(*S["gated"].at(f + 1))
                    if f >= 2:
                        dve.wait_ge(*S["act_used"].at(f - 1))
                    nc.vector.tensor_tensor(buf, core.ps[:, f % banks, 0:T], y, ALU.mult).then_inc(S["act_ready"].up(1), 1)
                else:
                    dve.wait_ge(*S["gated"].at(f + 1))
                    if gates is not None:
                        done(nc.vector.tensor_tensor(buf, buf, gates(f), ALU.mult))
                    nc.vector.tensor_tensor(buf, core.ps[:, f % banks, T:2 * T], buf, ALU.mult).then_inc(S["act_ready"].up(1), 1)
            dve.wait_ge(*S["act_used"].at(tiles))
            for m in range(KT):
                finish(dve, m, acc(m)).then_inc(S["chain"].up(1), 1)


def first_block(core, x, hall, mod, cond, ada_b, mods):
    nc = core.nc
    base = core.at
    g1 = core.take(KT, 2)
    prepare = core.counted("chain")
    with nc.Block(no_gpsimd_drain=True) as block:
        @block.vector
        def _(dve):
            done = Chain(dve, prepare)
            done(nc.vector.tensor_scalar(g1, mod[:, 8:16], 1.0, None, ALU.add))
            done(nc.vector.tensor_tensor(g1, g1, along(core.col("norm1_g"), 2), ALU.mult))
    gate = core.take(KT, T)
    gates = core.take(CHUNKS, 32)
    mark = core.at
    h = core.take(KT, TALL)
    mark_h = core.at
    sq, stat = core.take(KT, TALL), core.take(TALL)
    column_norm(core, "norm1", hall, h, sq, stat, EPS, lambda k: [
        (slice(0, TC), g1[:, k, 1:2], mod[:, k, 1:2]), (slice(TC, TALL), g1[:, k, 0:1], mod[:, k, 0:1])], False)
    core.at = mark_h
    q, k, v = core.take(HEADS, T), core.take(HEADS, TALL), core.take(HEADS, TALL)
    mark_qkv = core.at
    pad, taps = core.take(4, 2, T + 4), core.take(2, 2, T)
    gdn_project(core, h, q, k, v, gate, gates, pad, taps)
    core.at = mark_qkv
    mark_heads = core.at
    rq, rk = core.take(HEADS, T), core.take(HEADS, TALL)
    sq2 = core.take(2, TALL)
    inverse_norms(core, "qnorm", q, rq, sq2[:, :, 0:T], EPS, 1.0)
    inverse_norms(core, "knorm", k, rk, sq2, EPS, 1.0)
    normed = core.counted("qk_normed")
    with nc.Block(no_gpsimd_drain=True) as block:
        @block.vector
        def _(dve):
            nc.vector.tensor_tensor(q, q, rq, ALU.mult).then_inc(normed.up(1), 1)
            nc.vector.tensor_tensor(k, k, rk, ALU.mult).then_inc(normed.up(1), 1)
    core.at = mark_heads
    out = q
    beta, nbeta, kb_scale, kd_scale, alast, gc, g = (core.take(2, HEADS, CHUNKS) for _ in range(7))
    tmp = [core.take(2, HEADS, CHUNKS) for _ in range(3)] + [core.take(2 * HEADS)]
    gdn_gates(core, gates, beta, nbeta, kb_scale, kd_scale, alast, gc, g, tmp)
    gdn_heads(core, cond, ada_b, mods, q, k, v, beta, nbeta, kb_scale, kd_scale, alast, gc, g, out, h)
    core.at = mark_qkv
    ro, sq2, o = core.take(HEADS, T), core.take(2, T), core.take(HEADS, T)
    inverse_norms(core, "onorm", out, ro, sq2, EPS, float(P))
    gated = core.counted("chain")
    with nc.Block(no_gpsimd_drain=True) as block:
        @block.vector
        def _(dve):
            done = Chain(dve, gated)
            for hh in range(HEADS):
                done(nc.vector.tensor_tensor(o[:, hh], out[:, hh], ro[:, hh], ALU.mult))
                done(nc.vector.scalar_tensor_tensor(o[:, hh], o[:, hh], core.col("gdn_norm_g"), gate[:, hh], ALU.mult, ALU.mult))
    project(core, "gdn_out", o, D, lambda dve, f, sums: nc.vector.scalar_tensor_tensor(
        x[:, f], sums, mod[:, 16 + f, 0:1], x[:, f], ALU.mult, ALU.add))
    core.at = base
    g2 = core.take(KT)
    prepare2 = core.counted("chain")
    with nc.Block(no_gpsimd_drain=True) as block:
        @block.vector
        def _(dve):
            done = Chain(dve, prepare2)
            done(nc.vector.tensor_scalar(g2, mod[:, 32:40, 0], 1.0, None, ALU.add))
            done(nc.vector.tensor_tensor(g2, g2, core.col("norm2_g"), ALU.mult))
    h2, sq, stat = core.take(KT, T), core.take(KT, T), core.take(T)
    column_norm(core, "norm2", x, h2, sq, stat, EPS, lambda k: [(slice(0, T), g2[:, k:k + 1], mod[:, 24 + k, 0:1])], False)
    act_buf, pad, cv = core.take(2, T), core.take(2, T + 2), core.take(2, T)
    ffn(core, "conv_glu", h2, groups(FFN), act_buf, lambda dve, m, sums: nc.vector.scalar_tensor_tensor(
        x[:, m], sums, mod[:, 40 + m, 0:1], x[:, m], ALU.mult, ALU.add),
        (pad, core.col("ffn_conv_w", FFN_CONV, FT), core.col("ffn_conv_b"), cv))
    column_norm(core, "final", x, x, sq, stat, EPS, lambda k: [(slice(0, T), core.col("final_g")[:, k:k + 1], None)], False)
    core.at = base


def modulate(core, name, x, h, mod, scale_at, shift_at):
    nc = core.nc
    g = core.take(KT)
    chain = core.counted("chain")
    with nc.Block(no_gpsimd_drain=True) as block:
        @block.vector
        def _(dve):
            done = Chain(dve, chain)
            done(nc.vector.tensor_scalar(g, mod[:, scale_at:scale_at + KT, 0], 1.0, None, ALU.add))
            for k in range(KT):
                done(nc.vector.tensor_scalar(h[:, k], x[:, k], g[:, k:k + 1], mod[:, shift_at + k, 0:1], ALU.mult, ALU.add))
            done(nc.vector.tensor_scalar(x, x, ALPHA, None, ALU.mult))
            at = shift_at + 2 * KT
            done(nc.vector.tensor_scalar(mod[:, at:at + KT], mod[:, at:at + KT], 1.0, None, ALU.add))


def residual(core, x, mod, gate_at):
    nc = core.nc
    return lambda dve, f, sums: nc.vector.scalar_tensor_tensor(x[:, f], sums, mod[:, gate_at + f, 0:1], x[:, f], ALU.mult, ALU.add)


def layer_norm(core, name, x, which, sq, stat):
    g, b = core.col("ln_g", 4, KT), core.col("ln_b", 4, KT)
    column_norm(core, name, x, x, sq, stat, LN_EPS, lambda k: [(slice(0, T), g[:, which, k:k + 1], b[:, which, k:k + 1])], True)


def even_inputs(core, h, prow, qt, kt, vrow):
    nc, w = core.nc, core.w
    sums_ready, drained = core.counted("sums_ready"), core.counted("drained")
    with nc.Block(no_gpsimd_drain=True) as block:
        @block.sync
        def _(sp):
            w.issue(sp, w.taken + 3 + RING)

        @block.tensor
        def _(pe):
            tile = w.take(pe).rearrange("p (k c) -> p k c", k=KT)
            for s in range(2):
                for k in range(KT):
                    mm = nc.tensor.matmul(core.ps[:, s], h[:, k, s * P:(s + 1) * P], tile[:, k], start=(k == 0), stop=(k == KT - 1))
                mm.then_inc(sums_ready.up(1), 1)
            w.release()
            tile = w.take(pe).rearrange("p (k c) -> p k c", k=KT)
            for f in range(4):
                for k in range(KT):
                    mm = nc.tensor.matmul(core.ps[:, 2 + f, 0:T], tile[:, k, f * P:(f + 1) * P], h[:, k], start=(k == 0), stop=(k == KT - 1))
                    if k == 0:
                        w.tell(mm)
                mm.then_inc(sums_ready.up(1), 1)
            w.release()
            tile = w.take(pe)[:, 0:3 * P * KT].rearrange("p (k c) -> p k c", k=KT)
            for f in range(2):
                for k in range(KT):
                    mm = nc.tensor.matmul(core.ps[:, 6, f * T:(f + 1) * T], tile[:, k, f * P:(f + 1) * P], h[:, k], start=(k == 0), stop=(k == KT - 1))
                    if k == 0:
                        w.tell(mm)
            mm.then_inc(sums_ready.up(1), 1)
            for s in range(2):
                for k in range(KT):
                    mm = nc.tensor.matmul(core.ps[:, 7, s * P:(s + 1) * P], h[:, k, s * P:(s + 1) * P], tile[:, k, 2 * P:3 * P],
                                          start=(k == 0), stop=(k == KT - 1))
            mm.then_inc(sums_ready.up(1), 1)
            w.release()
            pe.wait_ge(*sums_ready.at(8))
            w.tell(pe.nop())

        @block.scalar
        def _(act):
            for s in range(2):
                act.wait_ge(*sums_ready.at(s + 1))
                nc.scalar.activation(prow[:, s], core.ps[:, s], ACT.Copy).then_inc(drained.up(1), 1)
            for f in range(4):
                act.wait_ge(*sums_ready.at(3 + f))
                nc.scalar.activation(qt[:, f], core.ps[:, 2 + f, 0:T], ACT.Copy, scale=HEAD ** -0.5).then_inc(drained.up(1), 1)
            act.wait_ge(*sums_ready.at(7))
            nc.scalar.activation(kt, core.ps[:, 6].rearrange("p (a b) -> p a b", a=2), ACT.Copy).then_inc(drained.up(1), 1)
            act.wait_ge(*sums_ready.at(8))
            nc.scalar.activation(vrow, core.ps[:, 7, 0:T].rearrange("p (a b) -> p a b", a=2), ACT.Copy).then_inc(drained.up(1), 1)


def pooling(core, prow, band, pooled, mix):
    nc = core.nc
    pool_ready, pool_sb, map_ready, mapped = (core.counted(s) for s in ("pool_ready", "pool_sb", "map_ready", "mapped"))
    pool_w, scale = core.col("pool_w", 4, P), core.col("pool_scale")
    with nc.Block(no_gpsimd_drain=True) as block:
        @block.tensor
        def _(pe):
            for g in range(4):
                for s in range(2):
                    mm = nc.tensor.matmul(core.ps[:, g, 0:T], prow[:, s, g * P:(g + 1) * P], band[:, g, s], start=(s == 0), stop=(s == 1))
                mm.then_inc(pool_ready.up(1), 1)
            for g in range(4):
                pe.wait_ge(*pool_sb.at(g + 1))
                nc.tensor.matmul(core.ps[:, 4 + g, 0:T], pool_w[:, g], pooled[:, g], start=True, stop=True).then_inc(map_ready.up(1), 1)

        @block.scalar
        def _(act):
            for g in range(4):
                act.wait_ge(*pool_ready.at(g + 1))
                nc.scalar.activation(pooled[:, g], core.ps[:, g, 0:T], ACT.Copy).then_inc(pool_sb.up(1), 1)

        @block.vector
        def _(dve):
            for g in range(4):
                dve.wait_ge(*map_ready.at(g + 1))
                nc.vector.tensor_scalar(mix[:, g], core.ps[:, 4 + g, 0:T], scale[:, g:g + 1], None, ALU.mult).then_inc(mapped.up(1), 1)


def attention(core, qt, kt, vrow, dist, mix):
    nc = core.nc
    S = {s: core.counted(s) for s in ("scores", "max", "exp", "probs", "probs_t", "probs_tsb", "out", "out_sb", "chain", "act_chain")}
    s_all, pt = core.take(2, 2, T), core.take(2, 2, T)
    m, total, edge = core.take(2, 2), core.take(2, 2), core.take(2, 2)
    sink = core.col("sink")

    def rows(h):
        return slice(HEAD * (h % 2), HEAD * (h % 2) + HEAD)

    with nc.Block(no_gpsimd_drain=True) as block:
        @block.tensor
        def _(pe):
            def scores(h):
                if h >= 2:
                    pe.wait_ge(*S["max"].at(h - 1))
                for b in range(2):
                    mm = nc.tensor.matmul(core.ps[:, h % 2, b * T:(b + 1) * T], qt[rows(h), h // 2, b * P:(b + 1) * P],
                                          kt[rows(h), h // (Q_HEADS // KV_HEADS)], start=True, stop=True)
                mm.then_inc(S["scores"].up(1), 1)

            scores(0)
            for h in range(Q_HEADS):
                if h + 1 < Q_HEADS:
                    scores(h + 1)
                pe.wait_ge(*S["probs"].at(h + 1))
                if h >= 2:
                    pe.wait_ge(*S["probs_tsb"].at(h - 1))
                for key in range(2):
                    for b in range(2):
                        tr = nc.tensor.transpose(core.ps[:, 2 + h % 2, key * T + b * P:key * T + (b + 1) * P],
                                                 s_all[:, h % 2, b, key * P:(key + 1) * P], core.const("ident"))
                tr.then_inc(S["probs_t"].up(1), 1)
                pe.wait_ge(*S["probs_tsb"].at(h + 1))
                if h >= 2:
                    pe.wait_ge(*S["out_sb"].at(h - 1))
                g = h // (Q_HEADS // KV_HEADS)
                for key in range(2):
                    mm = nc.tensor.matmul(core.ps[rows(h), 4 + h % 2, 0:T], vrow[:, key, g * HEAD:(g + 1) * HEAD], pt[:, h % 2, key],
                                          start=(key == 0), stop=(key == 1))
                mm.then_inc(S["out"].up(1), 1)

        @block.vector
        def _(dve):
            done = Chain(dve, S["chain"])
            for h in range(Q_HEADS):
                s = s_all[:, h % 2]
                dve.wait_ge(*S["scores"].at(h + 1))
                if h >= 2:
                    dve.wait_ge(*S["probs_t"].at(h - 1))
                done(nc.vector.scalar_tensor_tensor(s, dist, -SLOPES[h], core.ps[:, h % 2].rearrange("p (a b) -> p a b", a=2),
                                                    ALU.mult, ALU.add))
                mh = m[:, h % 2]
                done(nc.vector.tensor_reduce(mh, s, AX_X, ALU.max))
                nc.vector.tensor_scalar(mh, mh, sink[:, h:h + 1], -1.0, ALU.max, ALU.mult).then_inc(S["max"].up(1), 1)
                dve.wait_ge(*S["exp"].at(h + 1))
                th = total[:, h % 2]
                done(nc.vector.tensor_tensor(th, th, edge[:, h % 2], ALU.add))
                done(nc.vector.reciprocal(th, th))
                for b in range(2):
                    ins = nc.vector.tensor_scalar(s[:, b], s[:, b], th[:, b:b + 1], None, ALU.mult)
                ins.then_inc(S["probs"].up(1), 1)

        @block.scalar
        def _(act):
            done = Chain(act, S["act_chain"])

            def finish(h):
                act.wait_ge(*S["probs_t"].at(h + 1))
                if h >= 2:
                    act.wait_ge(*S["out"].at(h - 1))
                nc.scalar.activation(pt[:, h % 2], core.ps[:, 2 + h % 2].rearrange("p (a b) -> p a b", a=2), ACT.Copy).then_inc(S["probs_tsb"].up(1), 1)
                act.wait_ge(*S["out"].at(h + 1))
                nc.scalar.activation(mix[rows(h), 4 + h // 2], core.ps[rows(h), 4 + h % 2, 0:T], ACT.Copy).then_inc(S["out_sb"].up(1), 1)

            for h in range(Q_HEADS):
                act.wait_ge(*S["max"].at(h + 1))
                for b in range(2):
                    done(nc.scalar.activation(s_all[:, h % 2, b], s_all[:, h % 2, b], ACT.Exp, bias=m[:, h % 2, b:b + 1],
                                              accum_out=total[:, h % 2, b:b + 1]))
                nc.scalar.activation(edge[:, h % 2], m[:, h % 2], ACT.Exp, bias=sink[:, h:h + 1]).then_inc(S["exp"].up(1), 1)
                if h:
                    finish(h - 1)
            finish(Q_HEADS - 1)


def spatial_gate(core, u, v, vrow):
    nc = core.nc
    turned, rows_sb, mixed, biased, chain = (core.counted(s) for s in ("turned", "rows_sb", "mixed", "biased", "chain"))
    w_s, b_s = core.col("w_s", SG_GROUPS, P), core.col("b_s", SG_GROUPS, P)
    tmp = core.take(2, 2, P)
    with nc.Block(no_gpsimd_drain=True) as block:
        @block.tensor
        def _(pe):
            for g in range(SG_GROUPS):
                if g >= 4:
                    pe.wait_ge(*rows_sb.at(g - 3))
                for n in range(2):
                    tr = nc.tensor.transpose(core.ps[:, g % 4, n * P:(n + 1) * P], v[:, g, n * P:(n + 1) * P], core.const("ident"))
                tr.then_inc(turned.up(1), 1)
            for g in range(SG_GROUPS):
                pe.wait_ge(*rows_sb.at(g + 1))
                if g >= 4:
                    pe.wait_ge(*biased.at(g - 3))
                for n in range(2):
                    mm = nc.tensor.matmul(core.ps[:, 4 + g % 4, n * P:(n + 1) * P], vrow[:, g, n], w_s[:, g], start=True, stop=True)
                mm.then_inc(mixed.up(1), 1)

        @block.scalar
        def _(act):
            for g in range(SG_GROUPS):
                act.wait_ge(*turned.at(g + 1))
                nc.scalar.activation(vrow[:, g], core.ps[:, g % 4, 0:T].rearrange("p (a b) -> p a b", a=2), ACT.Copy).then_inc(rows_sb.up(1), 1)

        @block.vector
        def _(dve):
            for g in range(SG_GROUPS):
                dve.wait_ge(*mixed.at(g + 1))
                y = core.ps[:, 4 + g % 4, 0:T].rearrange("p (a b) -> p a b", a=2)
                nc.vector.tensor_tensor(tmp[:, g % 2], y, over(b_s[:, g], 2), ALU.add).then_inc(biased.up(1), 1)
                dve.wait_ge(*biased.at(g + 1))
                ug = u[:, g].rearrange("p (a b) -> p a b", a=2)
                nc.vector.tensor_tensor(ug, ug, tmp[:, g % 2], ALU.mult).then_inc(chain.up(1), 1)


def route(core, h, earlier, gates, place, rounds):
    nc = core.nc
    logits_ready, shifted, exp_ready, chosen, counted, chain = (
        core.counted(s) for s in ("logits_ready", "shifted", "exp_ready", "chosen", "numbered", "chain"))
    w_r = core.col("w_router", KT, EXPERTS)
    logits, rank, p = core.take(2, EXPERTS), core.take(2, EXPERTS), core.take(2, EXPERTS)
    beat, same = core.take(EXPERTS, EXPERTS), core.take(EXPERTS, EXPERTS)
    top, total, fullest = core.take(2), core.take(2), core.take(2)
    with nc.Block(no_gpsimd_drain=True) as block:
        @block.tensor
        def _(pe):
            for s in range(2):
                for k in range(KT):
                    mm = nc.tensor.matmul(core.ps[:, 0, s * EXPERTS:(s + 1) * EXPERTS], h[:, k, s * P:(s + 1) * P], w_r[:, k],
                                          start=(k == 0), stop=(k == KT - 1))
            mm.then_inc(logits_ready.up(1), 1)
            pe.wait_ge(*chosen.at(1))
            before, ones = core.const("strict1"), core.const("ones")
            for at, parts in enumerate((((before, 0),), ((ones, 0), (before, 1)), ((ones, 0), (ones, 1)))):
                for n, (m, s) in enumerate(parts):
                    mm = nc.tensor.matmul(core.ps[:, 1, at * EXPERTS:(at + 1) * EXPERTS], m, rank[:, s], start=(n == 0), stop=(n == len(parts) - 1))
            mm.then_inc(counted.up(1), 1)

        @block.vector
        def _(dve):
            done = Chain(dve, chain)
            dve.wait_ge(*logits_ready.at(1))
            done(nc.vector.tensor_copy(logits, core.ps[:, 0, 0:2 * EXPERTS].rearrange("p (a b) -> p a b", a=2)))
            done(nc.vector.tensor_reduce(top, logits, AX_X, ALU.max))
            nc.vector.tensor_tensor(p, logits, along(top, EXPERTS), ALU.subtract).then_inc(shifted.up(1), 1)
            for s in range(2):
                mine, other = along(logits[:, s], EXPERTS), over(logits[:, s], EXPERTS)
                done(nc.vector.tensor_tensor(same, other, mine, ALU.is_equal))
                done(nc.vector.tensor_tensor(same, same, earlier, ALU.mult))
                done(nc.vector.tensor_tensor(beat, other, mine, ALU.is_gt))
                done(nc.vector.tensor_tensor(beat, beat, same, ALU.add))
                done(nc.vector.tensor_reduce(rank[:, s], beat, AX_X, ALU.add))
            dve.wait_ge(*exp_ready.at(1))
            done(nc.vector.scalar_tensor_tensor(p, rank, 2.0, p, ALU.is_lt, ALU.mult))
            nc.vector.tensor_scalar(rank, rank, 2.0, None, ALU.is_lt).then_inc(chosen.up(1), 1)
            done(nc.vector.tensor_reduce(total, p, AX_X, ALU.add))
            done(nc.vector.reciprocal(total, total))
            done(nc.vector.tensor_tensor(gates, p, along(total, EXPERTS), ALU.mult))
            dve.wait_ge(*counted.at(1))
            done(nc.vector.tensor_scalar(rank, rank, -1e6, 1e6, ALU.mult, ALU.add))
            done(nc.vector.tensor_tensor(place, core.ps[:, 1, 0:2 * EXPERTS].rearrange("p (a b) -> p a b", a=2), rank, ALU.add))
            done(nc.vector.tensor_reduce(fullest[:, 0:1], core.ps[:, 1, 2 * EXPERTS:3 * EXPERTS], AX_X, ALU.max))
            done(nc.vector.tensor_scalar(rounds, fullest[:, 0:1], SLOTS + 0.5, 1.0, ALU.is_gt, ALU.add))

        @block.scalar
        def _(act):
            act.wait_ge(*shifted.at(1))
            nc.scalar.activation(p, p, ACT.Exp).then_inc(exp_ready.up(1), 1)


def token_rows(core, h, rows):
    nc = core.nc
    turned, copied = core.counted("turned"), core.counted("copied")
    with nc.Block(no_gpsimd_drain=True) as block:
        @block.tensor
        def _(pe):
            for n in range(4):
                for j in range(4):
                    k = 4 * (n % 2) + j
                    tr = nc.tensor.transpose(core.ps[:, n, j * P:(j + 1) * P], h[:, k, (n // 2) * P:(n // 2 + 1) * P], core.const("ident"))
                tr.then_inc(turned.up(1), 1)

        @block.scalar
        def _(act):
            for n in range(4):
                act.wait_ge(*turned.at(n + 1))
                nc.scalar.activation(rows[:, 2 * n:2 * n + 2].rearrange("p a b -> p (a b)"), core.ps[:, n], ACT.Copy).then_inc(copied.up(1), 1)


def experts(core, x, rows, h, act_buf, gates, place, rounds, slot_numbers, add):
    nc, w = core.nc, core.w
    S = {s: core.sem("moe_" + s) for s in (
        "give_ready", "take_ready", "give_turned", "give_copied", "gathered", "tokens_a", "tokens_b", "up_ready", "gated", "act_ready",
        "act_used", "down_ready", "rows_a", "rows_b", "scattered", "added", "extra_loaded5",
        "extra_loaded6")}
    C, FTE = SLOTS, EXPERT_FFN // P
    take_m = core.take(2, EXPERTS, C)
    give_m = h.rearrange("p k t -> p (k t)")[:, 0:2 * EXPERTS * C].rearrange("p (s e c) -> p s e c", s=2, e=EXPERTS)
    give_t = core.take(EXPERTS, T)
    xe, yrow = core.take(KT, C), core.take(D)
    assert core.at <= 32512 - 2 * TILE
    hrow = rows.rearrange("p (s k) t -> p s (k t)", s=2)
    ps, scatter_bank = core.ps, (6, 7, 4, 5)
    first = w.issued - RING
    assert w.taken == first
    slot_of, before = [], []
    for j in range(MOE_RING):
        slot_of.append((first + j) % RING if j < RING else j)
        before.append((first + RING - 1 - slot_of[j]) // RING if j < RING else 0)
    loaded = w.tile_loaded + [S["extra_loaded5"], S["extra_loaded6"]]

    def slot(j):
        s = slot_of[j]
        return w.ring[:, s, :] if s < RING else core.arena[:, 32512 - (MOE_RING - s) * TILE:32512 - (MOE_RING - s - 1) * TILE]

    def rounds_of(eng):
        return eng.value_load(rounds[0:1, 0:1], min_val=1, max_val=-(-T // SLOTS))

    with nc.Block(no_gpsimd_drain=True) as block:
        @block.sync
        def _(sp):
            n_rounds = rounds_of(sp)

            def load(i, number, turn):
                if turn is not None:
                    sp.wait_ge(w.tile_used, first + turn * EXPERT_TILES + i - MOE_RING + 1)
                sp.dma_start(slot(i % MOE_RING), w.dram[bass.ds(number, 1)].rearrange("n p c -> p (n c)")).then_inc(loaded[slot_of[i % MOE_RING]], 16)

            for i in range(RING, EXPERT_TILES):
                load(i, first + i, None if i < MOE_RING else 0)
            with sp.Fori(1, EXPERTS) as e:
                for i in range(EXPERT_TILES):
                    load(i, e * EXPERT_TILES + first + i, e)
            with sp.If(n_rounds > 1):
                with sp.Fori(1, n_rounds) as r:
                    with sp.Fori(0, EXPERTS) as e:
                        for i in range(EXPERT_TILES):
                            load(i, e * EXPERT_TILES + first + i, r * EXPERTS + e)
            sp.nop()

        @block.tensor
        def _(pe):
            def take_tile(i, turn):
                pe.wait_ge(loaded[slot_of[i % MOE_RING]], turn * (16 * EXPERT_TILES // MOE_RING) + 16 * (before[i % MOE_RING] + i // MOE_RING + 1))
                return slot(i % MOE_RING)

            def gather(e):
                for k in range(KT):
                    for s in range(2):
                        mm = nc.tensor.matmul(ps[:, 4 + k // 4, (k % 4) * C:(k % 4 + 1) * C], hrow[:, s, k * P:(k + 1) * P],
                                              take_m[:, s, bass.ds(e, 1), :].rearrange("p e c -> p (e c)"), start=(s == 0), stop=(s == 1))
                    if k % 4 == 3:
                        mm.then_inc(S["gathered"], 1)

            def expert(r, e, last=False):
                turn = r * EXPERTS + e
                pe.wait_ge(S["tokens_a"], turn + 1)
                pe.wait_ge(S["tokens_b"], turn + 1)

                def up(f, gate_w, up_w):
                    j = f % 4
                    if f >= 2:
                        pe.wait_ge(S["act_ready"], turn * FTE + (f - 1))
                    for half, tile in ((0, gate_w), (1, up_w)):
                        for k in range(KT):
                            mm = nc.tensor.matmul(ps[:, f % 2, half * C:(half + 1) * C], tile[:, k, j * P:(j + 1) * P], xe[:, k],
                                                  start=(k == 0), stop=(k == KT - 1))
                            if k == 0:
                                w.tell(mm)
                    mm.then_inc(S["up_ready"], 1)
                    if j == 3:
                        w.release(2)

                def down(f, tile):
                    pe.wait_ge(S["act_ready"], turn * FTE + (f + 1))
                    for half in range(2):
                        mm = nc.tensor.matmul(ps[0:C, 2 + half], act_buf[:, f % 2, 0:C], tile[:, f % 4, half * 512:(half + 1) * 512],
                                              start=(f == 0), stop=(f == FTE - 1))
                        if half == 0:
                            w.tell(mm)
                    mm.then_inc(S["act_used"] if f < FTE - 1 else S["down_ready"], 1)
                    if f % 4 == 3:
                        w.release()

                down_w = None
                for f in range(FTE):
                    if f % 4 == 0:
                        gate_w = take_tile(f // 4 * 3, turn).rearrange("p (k c) -> p k c", k=KT)
                        up_w = take_tile(f // 4 * 3 + 1, turn).rearrange("p (k c) -> p k c", k=KT)
                    up(f, gate_w, up_w)
                    if f:
                        down(f - 1, down_w)
                    if f % 4 == 0:
                        down_w = take_tile(f // 4 * 3 + 2, turn).rearrange("p (j c) -> p j c", j=4)
                down(FTE - 1, down_w)
                pe.wait_ge(S["added"], turn * 4 + 1)
                if not last:
                    gather(e + 1)
                for m in range(KT):
                    if m == 0:
                        pe.wait_ge(S["rows_a"], turn + 1)
                    if m == 4:
                        pe.wait_ge(S["rows_b"], turn + 1)
                        if not last:
                            pe.wait_ge(S["tokens_a"], turn + 2)
                            pe.wait_ge(S["tokens_b"], turn + 2)
                    mm = nc.tensor.matmul(ps[:, scatter_bank[m // 2], (m % 2) * T:(m % 2 + 1) * T], yrow[0:C, m * P:(m + 1) * P],
                                          give_t[0:C, bass.ds(e, 1), :].rearrange("p e t -> p (e t)"), start=True, stop=True)
                    if m == 0:
                        w.tell(mm)
                    if m % 2:
                        mm.then_inc(S["scattered"], 1)

            with pe.Fori(0, rounds_of(pe)) as r:
                pe.wait_ge(S["added"], r * (4 * EXPERTS) + 1)
                pe.wait_ge(S["give_ready"], r + 1)
                for e in range(EXPERTS):
                    if e >= 4:
                        pe.wait_ge(S["give_copied"], r * EXPERTS + (e - 3))
                    for s in range(2):
                        tr = nc.tensor.transpose(ps[0:C, e % 4, s * P:(s + 1) * P], give_m[:, s, e], core.const("ident"))
                    tr.then_inc(S["give_turned"], 1)
                pe.wait_ge(S["give_copied"], r * EXPERTS + EXPERTS)
                pe.wait_ge(S["take_ready"], r + 1)
                gather(0)
                with pe.Fori(0, EXPERTS - 1) as e:
                    expert(r, e)
                expert(r, EXPERTS - 1, last=True)

        @block.scalar
        def _(act):
            def take_tokens(turn):
                act.wait_ge(S["gathered"], turn * 2 + 1)
                nc.scalar.activation(xe[:, 0:4].rearrange("p k c -> p (k c)"), ps[:, 4, 0:4 * C], ACT.Copy).then_inc(S["tokens_a"], 1)

            def expert(turn, last=False):
                for f in range(FTE):
                    act.wait_ge(S["up_ready"], turn * FTE + (f + 1))
                    if f >= 2:
                        act.wait_ge(S["act_used"], turn * (FTE - 1) + (f - 1))
                    nc.scalar.activation(act_buf[:, f % 2, 0:C], ps[:, f % 2, 0:C], ACT.Silu).then_inc(S["gated"], 1)
                act.wait_ge(S["down_ready"], turn + 1)
                nc.scalar.activation(yrow[0:C, 0:512], ps[0:C, 2], ACT.Copy).then_inc(S["rows_a"], 1)
                if not last:
                    take_tokens(turn + 1)

            with act.Fori(0, rounds_of(act)) as r:
                for e in range(EXPERTS):
                    act.wait_ge(S["give_turned"], r * EXPERTS + (e + 1))
                    nc.scalar.activation(give_t[0:C, e], ps[0:C, e % 4, 0:T], ACT.Copy).then_inc(S["give_copied"], 1)
                take_tokens(r * EXPERTS)
                with act.Fori(0, EXPERTS - 1) as e:
                    expert(r * EXPERTS + e)
                expert(r * EXPERTS + EXPERTS - 1, last=True)

        @block.vector
        def _(dve):
            def take_tokens(turn):
                dve.wait_ge(S["gathered"], turn * 2 + 2)
                nc.vector.tensor_copy(xe[:, 4:8].rearrange("p k c -> p (k c)"), ps[:, 5, 0:4 * C]).then_inc(S["tokens_b"], 1)

            def expert(turn, last=False):
                for f in range(FTE):
                    dve.wait_ge(S["gated"], turn * FTE + (f + 1))
                    b = act_buf[:, f % 2, 0:C]
                    nc.vector.tensor_tensor(b, ps[:, f % 2, C:2 * C], b, ALU.mult).then_inc(S["act_ready"], 1)
                dve.wait_ge(S["down_ready"], turn + 1)
                nc.vector.tensor_copy(yrow[0:C, 512:1024], ps[0:C, 3]).then_inc(S["rows_b"], 1)
                if not last:
                    take_tokens(turn + 1)
                for m in range(KT):
                    if m % 2 == 0:
                        dve.wait_ge(S["scattered"], turn * 4 + (m // 2 + 1))
                    ins = add(dve, m, ps[:, scatter_bank[m // 2], (m % 2) * T:(m % 2 + 1) * T])
                    if m % 2:
                        ins.then_inc(S["added"], 1)

            nc.vector.memset(xe[:, 0, 0:1], 0.0).then_inc(S["added"], 1)
            with dve.Fori(0, rounds_of(dve)) as r:
                dve.wait_ge(S["added"], r * (4 * EXPERTS) + 1)
                for s in range(2):
                    for e in range(EXPERTS):
                        last = nc.vector.tensor_scalar(give_m[:, s, e], slot_numbers, place[:, s, e:e + 1], gates[:, s, e:e + 1],
                                                       ALU.is_equal, ALU.mult)
                last.then_inc(S["give_ready"], 1)
                for s in range(2):
                    for e in range(EXPERTS):
                        last = nc.vector.tensor_scalar(take_m[:, s, e], slot_numbers, place[:, s, e:e + 1], None, ALU.is_equal)
                last.then_inc(S["take_ready"], 1)
                dve.wait_ge(S["take_ready"], r + 1)
                nc.vector.tensor_scalar(place, place, -float(C), None, ALU.add)
                take_tokens(r * EXPERTS)
                with dve.Fori(0, EXPERTS - 1) as e:
                    expert(r * EXPERTS + e)
                expert(r * EXPERTS + EXPERTS - 1, last=True)


def second_block(core, x, mods, consts2):
    nc = core.nc
    base = core.at
    band = consts2[:, 0:8 * T].rearrange("p (g s t) -> p g s t", g=4, s=2)
    dist = consts2[:, 8 * T:10 * T].rearrange("p (a b) -> p a b", a=2)
    earlier = consts2[:, 10 * T:10 * T + EXPERTS ** 2].rearrange("p (a b) -> p a b", a=EXPERTS)
    slot_numbers = consts2[:, 10 * T + EXPERTS ** 2:]
    h, sq, stat = core.take(KT, T), core.take(KT, T), core.take(T)
    act_buf = core.take(2, T)
    mark = core.at

    modulate(core, "even", x, h, mods[0], 8, 0)
    prow, qt, kt, vrow, mix = core.take(2, 512), core.take(4, T), core.take(2, T), core.take(2, P), core.take(KT, T)
    pooled = core.take(4, T)
    even_inputs(core, h, prow, qt, kt, vrow)
    pooling(core, prow, band, pooled, mix)
    attention(core, qt, kt, vrow, dist, mix)
    project(core, "even_out", mix, D, residual(core, x, mods[0], 16))
    layer_norm(core, "ln00", x, 0, sq, stat)
    core.at = mark
    modulate(core, "swiglu_in", x, h, mods[0], 32, 24)
    ffn(core, "swiglu", h, groups(FFN), act_buf, residual(core, x, mods[0], 40))
    layer_norm(core, "ln01", x, 1, sq, stat)

    modulate(core, "odd", x, h, mods[1], 8, 0)
    u, v, vr = core.take(KT, T), core.take(KT, T), core.take(SG_GROUPS, 2, P)
    project(core, "odd_in", h, 2 * D, lambda act, f, sums: nc.scalar.activation(
        (u if f < KT else v)[:, f % KT], sums, ACT.Gelu_apprx_tanh), on="scalar")
    column_norm(core, "sg_norm", v, v, sq, stat, LN_EPS, lambda k: [
        (slice(0, T), core.col("sg_g")[:, k:k + 1], core.col("sg_b")[:, k:k + 1])], True)
    spatial_gate(core, u, v, vr)
    project(core, "odd_out", u, D, residual(core, x, mods[1], 16))
    layer_norm(core, "ln10", x, 2, sq, stat)
    core.at = mark
    modulate(core, "moe_in", x, h, mods[1], 32, 24)
    gates, place, rounds = core.take(2, EXPERTS), core.take(2, EXPERTS), core.take(1).bitcast(I32)
    route(core, h, earlier, gates, place, rounds)
    token_rows(core, h, sq)
    experts(core, x, sq, h, act_buf, gates, place, rounds, slot_numbers, residual(core, x, mods[1], 40))
    layer_norm(core, "ln11", x, 3, sq, stat)
    core.at = base


def program(nc, tokens, params, params2, consts, consts2, weights, out):
    with ExitStack() as ctx:
        core = Core(nc, ctx, weights, stream_plan())
        x = core.take(KT, T)
        cond = core.take(KT, 3)
        mod, *mods = core.take(48, 2), core.take(48, 1), core.take(48, 1)
        ada_b = core.take(DEPTH_2 * 48)
        mark = core.at
        core.cols, core.cols_of = core.take(N_COLS), COLS
        hall = core.arena[:, 32512 - KT * TALL:32512].rearrange("p (k t) -> p k t", k=KT)
        load_inputs(core, [(core.cols, params), (core.consts, consts), (hall, tokens), (x, tokens[:, :, TC:TALL]),
                           (ada_b, params2[:, COLS_2["ada_b"]])])
        silu_done = core.counted("cond_silu_done")
        with nc.Block(no_gpsimd_drain=True) as block:
            @block.scalar
            def _(act):
                nc.scalar.activation(cond, core.col("cond", KT, 3), ACT.Silu).then_inc(silu_done.up(1), 1)
        conditioning(core, cond, core.col("b_mod"), mod)
        first_block(core, x, hall, mod, cond, ada_b, mods)
        core.at = mark
        core.cols, core.cols_of = core.take(N_COLS_2), COLS_2
        c2 = core.take(N_CONSTS_2)
        landed = core.sem("inputs2_landed")
        with nc.Block(no_gpsimd_drain=True) as block:
            @block.scalar
            def _(act):
                act.dma_start(core.cols, params2).then_inc(landed, 16)
                act.dma_start(c2, consts2).then_inc(landed, 16)
                act.wait_ge(landed, 32)
        second_block(core, x, mods, c2)
        stored = core.sem("out_stored")
        with nc.Block(no_gpsimd_drain=True) as block:
            @block.sync
            def _(sp):
                sp.dma_start(out, x).then_inc(stored, 16)
                sp.wait_ge(stored, 16)



def columns(a):
    a = np.ascontiguousarray(a)
    return a.reshape(-1, P).T


def rows_tile(w):
    return w.reshape(w.shape[0] // P, P, w.shape[1]).transpose(1, 0, 2).reshape(P, -1)


def everywhere(a):
    return np.broadcast_to(np.asarray(a).reshape(1, -1), (P, np.asarray(a).size))


def kernel(**inputs):
    import concourse.bacc as bacc
    from concourse.bass_utils import run_bass_kernel_spmd as run

    a = {k: np.asarray(v) for k, v in inputs.items()}
    cond = np.stack([a["c"][0], a["c_ctx"], a["c_2"][0]], axis=-1)
    pieces = dict(cond=rows_tile(cond), b_mod=columns(a["b_mod"]), norm1_g=columns(a["norm1_g"]), norm2_g=columns(a["norm2_g"]),
                  final_g=columns(a["final_norm_g"]), conv_w=columns(a["gdn_conv_w"]), ffn_conv_w=columns(a["ffn_conv_w"]),
                  ffn_conv_b=columns(a["ffn_conv_b"]), gdn_norm_g=columns(a["gdn_norm_g"]), a_log=everywhere(a["gdn_a_log"]),
                  dt_bias=everywhere(a["gdn_dt_bias"]), w_ba=rows_tile(a["gdn_w_in"][0][:, 4 * D:]))
    params = np.concatenate([pieces[k] for k in PARAMS_1], axis=1)
    kv = a["ev_w_in_2"][0][:, D:]
    pieces = dict(ada_b=columns(a["ada_b_2"]), ln_g=columns(a["ln_g_2"]), ln_b=columns(a["ln_b_2"]), pool_scale=columns(a["ev_pool_scale_2"]),
                  sink=everywhere(a["ev_sink_2"]), sg_g=columns(a["od_sg_ln_g_2"]), sg_b=columns(a["od_sg_ln_b_2"]),
                  b_s=everywhere(a["od_b_s_2"]), w_s=a["od_w_s_2"][0].transpose(2, 0, 1).reshape(P, -1),
                  pool_w=a["ev_pool_w_2"][0].transpose(1, 0, 2).reshape(P, -1), w_router=rows_tile(a["moe_w_router_2"][0]))
    params2 = np.concatenate([pieces[k] for k in PARAMS_2], axis=1)
    tokens = np.concatenate([a["ctx"][0], a["x"][0]]).T
    tokens = rows_tile(tokens).reshape(P, KT, TALL)
    tiles = []

    def stream(block):
        t = np.zeros((P, TILE), np.float32)
        t[:, :block.shape[1]] = block
        tiles.append(t)

    def stream_columns(w):
        for c, n in groups(w.shape[1]):
            stream(rows_tile(w[:, c:c + n]))

    def stream_ffn(first, second, down):
        for c, n in groups(first.shape[1]):
            stream(rows_tile(first[:, c:c + n]))
            stream(rows_tile(second[:, c:c + n]))
            stream(rows_tile(down[c:c + n]))

    stream_columns(a["w_mod"][0])
    stream_columns(a["gdn_w_in"][0][:, :4 * D])
    stream_columns(a["ada_w_2"][0])
    stream_columns(a["ada_w_2"][1])
    stream_columns(a["gdn_w_out"][0])
    stream_ffn(a["ffn_w_in"][0][:, :FFN], a["ffn_w_in"][0][:, FFN:], a["ffn_w_out"][0])
    stream_columns(a["ev_w_in_2"][0][:, :D])
    stream(rows_tile(np.concatenate([kv[:, 0:64], kv[:, 0:64], kv[:, 64:128], kv[:, 64:128], kv[:, 128:256]], axis=1)))
    stream_columns(a["ev_w_out_2"][0])
    stream_ffn(a["ffn_w_gate_2"][0], a["ffn_w_up_2"][0], a["ffn_w_down_2"][0])
    stream_columns(a["od_w_in_2"][0])
    stream_columns(a["od_w_out_2"][0])
    for e in range(EXPERTS):
        stream_ffn(a["moe_w_gate_2"][0, e], a["moe_w_up_2"][0, e], a["moe_w_down_2"][0, e])
    sent = dict(tokens=tokens, params=params, params2=params2, consts=constants(), consts2=constants_2(), weights=np.stack(tiles))
    nc = bacc.Bacc("TRN2", target_bir_lowering=False, num_devices=1)
    sent = {k: np.ascontiguousarray(v) for k, v in sent.items()}
    aps = [nc.dram_tensor(k, v.shape, F32, kind="ExternalInput").ap() for k, v in sent.items()]
    out = nc.dram_tensor("out", (P, KT, T), F32, kind="ExternalOutput").ap()
    program(nc, *aps, out)
    r = run(nc, [sent], core_ids=[0])
    got = r.results[0]["out"]
    return np.ascontiguousarray(got.transpose(2, 1, 0).reshape(1, T, D))
```
